# Optimizing a Trainium2 kernel written in Bass

```python
import jax, jax.numpy as jnp
from jax import lax
import numpy as np

D_MODEL = 1024
BATCH = 1
SEQ = 512
DEPTH = 2

MLA_HEADS = 8
MLA_Q_LORA = 256
MLA_KV_LORA = 128
MLA_NOPE = 64
MLA_ROPE = 32
MLA_V = 64
SWA_HEADS = 8
SWA_KV_HEADS = 2
SWA_HEAD_DIM = 64
SWA_WINDOW = 128
SB_HEADS = 8
SB_HEAD_DIM = 64
D_FF = 4 * D_MODEL
BLOCK = 128
ROPE_THETA = 10000.0
EPS = 1e-6
N_BRANCHES = 3
MIX_A = MLA_HEADS * MLA_V
MIX_B = SWA_HEADS * SWA_HEAD_DIM
MIX_C = SB_HEADS * SB_HEAD_DIM

SPLIT_SIZES = (
    MLA_Q_LORA, MLA_KV_LORA, MLA_ROPE,
    SWA_HEADS * SWA_HEAD_DIM, SWA_KV_HEADS * SWA_HEAD_DIM, SWA_KV_HEADS * SWA_HEAD_DIM,
    SB_HEADS * SB_HEAD_DIM, SB_HEADS * SB_HEAD_DIM, SB_HEADS * SB_HEAD_DIM,
    N_BRANCHES * D_MODEL,
)
IN_WIDTH = sum(SPLIT_SIZES)
SPLIT_POINTS = [int(v) for v in np.cumsum(SPLIT_SIZES)[:-1]]

kernel_name = "hybrid_mla_swa_sinks_stickbreak_gated"

def rms_norm(x, g):
    xf = x.astype(jnp.float32)
    y = xf * lax.rsqrt(jnp.mean(xf * xf, axis=-1, keepdims=True) + EPS)
    return (y * g.astype(jnp.float32)).astype(x.dtype)

def rope(x, positions):
    d = x.shape[-1]
    inv = 1.0 / (ROPE_THETA ** (jnp.arange(0, d, 2, dtype=jnp.float32) / d))
    ang = positions.astype(jnp.float32)[..., None] * inv
    cos = jnp.cos(ang)[:, :, None, :]
    sin = jnp.sin(ang)[:, :, None, :]
    xf = x.astype(jnp.float32)
    x1, x2 = xf[..., : d // 2], xf[..., d // 2:]
    return jnp.concatenate([x1 * cos - x2 * sin, x2 * cos + x1 * sin], axis=-1).astype(x.dtype)

def to_blocks(t):
    b, s = t.shape[:2]
    return jnp.moveaxis(t.reshape(b, s // BLOCK, BLOCK, *t.shape[2:]), 1, 0)

def from_blocks(t):
    t = jnp.moveaxis(t, 0, 1)
    return t.reshape(t.shape[0], t.shape[1] * t.shape[2], *t.shape[3:])

def mla_branch(c_q, c_kv, k_rope, positions, g_q_lat, g_kv_lat, w_uq, w_ukv):
    B, S, _ = c_q.shape
    q = (rms_norm(c_q, g_q_lat) @ w_uq).reshape(B, S, MLA_HEADS, MLA_NOPE + MLA_ROPE)
    q_nope = q[..., :MLA_NOPE]
    q_pe = rope(q[..., MLA_NOPE:], positions)
    kv = (rms_norm(c_kv, g_kv_lat) @ w_ukv).reshape(B, S, MLA_HEADS, MLA_NOPE + MLA_V)
    k_nope, v = kv[..., :MLA_NOPE], kv[..., MLA_NOPE:]
    k_pe = rope(k_rope[:, :, None, :], positions)[:, :, 0]
    scale = (MLA_NOPE + MLA_ROPE) ** -0.5
    key_pos = jnp.arange(S)

    def block(args):
        qn, qp, i = args
        s = (jnp.einsum('bqhd,bkhd->bhqk', qn, k_nope, preferred_element_type=jnp.float32)
             + jnp.einsum('bqhd,bkd->bhqk', qp, k_pe, preferred_element_type=jnp.float32)) * scale
        q_pos = i * BLOCK + jnp.arange(BLOCK)
        s = jnp.where(key_pos[None, :] <= q_pos[:, None], s, -jnp.inf)
        p = jax.nn.softmax(s, axis=-1).astype(v.dtype)
        return jnp.einsum('bhqk,bkhd->bqhd', p, v)

    out = lax.map(block, (to_blocks(q_nope), to_blocks(q_pe), jnp.arange(S // BLOCK)))
    return from_blocks(out).reshape(B, S, MIX_A)

def swa_branch(q, k, v, positions, sinks):
    B, S, _ = q.shape
    G = SWA_HEADS // SWA_KV_HEADS
    n = S // BLOCK
    q = rope(q.reshape(B, S, SWA_HEADS, SWA_HEAD_DIM), positions)
    k = rope(k.reshape(B, S, SWA_KV_HEADS, SWA_HEAD_DIM), positions)
    v = v.reshape(B, S, SWA_KV_HEADS, SWA_HEAD_DIM)
    qb = q.reshape(B, n, BLOCK, SWA_KV_HEADS, G, SWA_HEAD_DIM)

    def band(t):
        tb = t.reshape(B, n, BLOCK, *t.shape[2:])
        prev = jnp.pad(tb, ((0, 0), (1, 0), (0, 0), (0, 0), (0, 0)))[:, :-1]
        return jnp.concatenate([prev, tb], axis=2)

    kb, vb = band(k), band(v)
    s = jnp.einsum('bnqkgd,bnskd->bnkgqs', qb, kb, preferred_element_type=jnp.float32) * SWA_HEAD_DIM ** -0.5
    qi = jnp.arange(BLOCK)[:, None] + BLOCK
    si = jnp.arange(2 * BLOCK)[None, :]
    diff = qi - si
    valid = (diff >= 0) & (diff < SWA_WINDOW)
    blk = jnp.arange(n)
    valid = valid[None] & ((blk[:, None, None] > 0) | (si[None] >= BLOCK))
    s = jnp.where(valid[None, :, None, None], s, -jnp.inf)
    sink = sinks.astype(jnp.float32).reshape(SWA_KV_HEADS, G)[None, None, :, :, None, None]
    m = jnp.maximum(jnp.max(s, axis=-1, keepdims=True), sink)
    p = jnp.exp(s - m)
    p = (p / (jnp.sum(p, axis=-1, keepdims=True) + jnp.exp(sink - m))).astype(v.dtype)
    o = jnp.einsum('bnkgqs,bnskd->bnqkgd', p, vb)
    return o.reshape(B, S, MIX_B)

def stick_breaking_branch(q, k, v):
    B, S, _ = q.shape
    q = q.reshape(B, S, SB_HEADS, SB_HEAD_DIM)
    k = k.reshape(B, S, SB_HEADS, SB_HEAD_DIM)
    v = v.reshape(B, S, SB_HEADS, SB_HEAD_DIM)
    scale = SB_HEAD_DIM ** -0.5
    key_pos = jnp.arange(S)

    def block(args):
        qb, i = args
        z = jnp.einsum('bqhd,bkhd->bhqk', qb, k, preferred_element_type=jnp.float32) * scale
        q_pos = i * BLOCK + jnp.arange(BLOCK)
        before = key_pos[None, :] < q_pos[:, None]
        log_1m_beta = jnp.where(before, jax.nn.log_sigmoid(-z), 0.0)
        tail = lax.cumsum(log_1m_beta, axis=3, reverse=True) - log_1m_beta
        a = jnp.where(before, jnp.exp(jax.nn.log_sigmoid(z) + tail), 0.0).astype(v.dtype)
        return jnp.einsum('bhqk,bkhd->bqhd', a, v)

    out = lax.map(block, (to_blocks(q), jnp.arange(S // BLOCK)))
    return from_blocks(out).reshape(B, S, MIX_C)

def hybrid_layer(x, positions, g_mix_pre, w_in, b_gate, g_q_lat, g_kv_lat, w_uq, w_ukv, swa_sinks,
                 w_o_mla, w_o_swa, w_o_sb, w_out, g_mix_post, g_mlp_pre, w_up, w_down, g_mlp_post):
    B, S, D = x.shape
    h = rms_norm(x, g_mix_pre)
    proj = h @ w_in
    (c_q, c_kv, k_rope, q_swa, k_swa, v_swa, q_sb, k_sb, v_sb, gate_logits) = jnp.split(proj, SPLIT_POINTS, axis=-1)
    o_a = mla_branch(c_q, c_kv, k_rope, positions, g_q_lat, g_kv_lat, w_uq, w_ukv) @ w_o_mla
    o_b = swa_branch(q_swa, k_swa, v_swa, positions, swa_sinks) @ w_o_swa
    o_c = stick_breaking_branch(q_sb, k_sb, v_sb) @ w_o_sb
    gates = jax.nn.sigmoid((gate_logits + b_gate).astype(jnp.float32)).astype(x.dtype)
    gates = gates.reshape(B, S, N_BRANCHES, D)
    mixed = gates[:, :, 0] * o_a + gates[:, :, 1] * o_b + gates[:, :, 2] * o_c
    x = x + rms_norm(mixed @ w_out, g_mix_post)
    h = rms_norm(x, g_mlp_pre)
    u = jnp.square(jax.nn.relu(h @ w_up))
    return x + rms_norm(u @ w_down, g_mlp_post)

def setup_inputs(seed: int = 0) -> dict:
    key = jax.random.key(seed)
    ks = jax.random.split(key, 24)
    f32 = jnp.float32

    def dense(k, fan_in, fan_out):
        return jax.random.normal(k, (DEPTH, fan_in, fan_out), f32) * fan_in ** -0.5

    def gain(k, n):
        return 1.0 + 0.05 * jax.random.normal(k, (DEPTH, n), f32)

    x = jax.random.normal(ks[0], (BATCH, SEQ, D_MODEL), f32)
    start = jax.random.randint(ks[1], (BATCH, 1), 0, 1024, dtype=jnp.int32)
    positions = start + jnp.arange(SEQ, dtype=jnp.int32)[None, :]
    return {
        "x": x,
        "positions": positions,
        "g_mix_pre": gain(ks[2], D_MODEL),
        "w_in": dense(ks[3], D_MODEL, IN_WIDTH),
        "b_gate": 0.02 * jax.random.normal(ks[4], (DEPTH, N_BRANCHES * D_MODEL), f32),
        "g_q_lat": gain(ks[5], MLA_Q_LORA),
        "g_kv_lat": gain(ks[6], MLA_KV_LORA),
        "w_uq": dense(ks[7], MLA_Q_LORA, MLA_HEADS * (MLA_NOPE + MLA_ROPE)),
        "w_ukv": dense(ks[8], MLA_KV_LORA, MLA_HEADS * (MLA_NOPE + MLA_V)),
        "swa_sinks": 0.5 * jax.random.normal(ks[9], (DEPTH, SWA_HEADS), f32),
        "w_o_mla": dense(ks[10], MIX_A, D_MODEL),
        "w_o_swa": dense(ks[11], MIX_B, D_MODEL),
        "w_o_sb": dense(ks[12], MIX_C, D_MODEL),
        "w_out": dense(ks[13], D_MODEL, D_MODEL),
        "g_mix_post": gain(ks[14], D_MODEL),
        "g_mlp_pre": gain(ks[15], D_MODEL),
        "w_up": dense(ks[16], D_MODEL, D_FF),
        "w_down": dense(ks[17], D_FF, D_MODEL),
        "g_mlp_post": gain(ks[18], D_MODEL),
    }

def reference(x, positions, g_mix_pre, w_in, b_gate, g_q_lat, g_kv_lat, w_uq, w_ukv, swa_sinks,
              w_o_mla, w_o_swa, w_o_sb, w_out, g_mix_post, g_mlp_pre, w_up, w_down, g_mlp_post):
    for l in range(DEPTH):
        x = hybrid_layer(x, positions, g_mix_pre[l], w_in[l], b_gate[l], g_q_lat[l], g_kv_lat[l],
                         w_uq[l], w_ukv[l], swa_sinks[l], w_o_mla[l], w_o_swa[l], w_o_sb[l], w_out[l],
                         g_mix_post[l], g_mlp_pre[l], w_up[l], w_down[l], g_mlp_post[l])
    return x


_drawn_inputs = setup_inputs


def setup_inputs(seed=0):
    import zlib

    import numpy as np

    out = dict(_drawn_inputs(seed))
    spreads = {}
    factors = {'b_gate': 7.508, 'g_q_lat': 5.988, 'g_kv_lat': 3.084, 'swa_sinks': 7.632}
    for name, (base, spread) in spreads.items():
        noise = np.random.default_rng([zlib.crc32(name.encode()), seed]).standard_normal(out[name].shape)
        drawn = base * np.exp(spread * noise) if base else spread * noise
        out[name] = __import__('jax').numpy.asarray(drawn.astype(out[name].dtype))
    for name, factor in factors.items():
        out[name] = (out[name] * factor).astype(out[name].dtype)
    return out
```

```python
from contextlib import ExitStack

import concourse.bass as bass
import numpy as np
from concourse import mybir

ALU = mybir.AluOpType
ACT = mybir.ActivationFunctionType
F32 = mybir.dt.float32
F32R = mybir.dt.float32r
I32 = mybir.dt.int32

P = 128
DEPTH, D, SEQ = 2, 1024, 512
HEADS, HEAD = 8, 64
ROPE_DIM, Q_LORA, KV_LORA = 32, 256, 128
D_FF = 4096
WINDOW = 128
EPS = 1e-6
THETA = 10000.0
KT = D // P
NB = SEQ // P
PAIRS = HEADS // 2
CH = KT * P
GROUPS = D_FF // D

C_LATENT = 0
C_MLA = C_LATENT + 4
C_SWA = C_MLA + PAIRS
C_SB = C_SWA + 2 + PAIRS
C_MERGE = C_SB + 3 * PAIRS
C_OUT = C_MERGE + 9 * (KT // 2)
C_MLP = C_OUT + KT
CHUNKS = C_MLP + 2 * KT * GROUPS
RING = 3
CHUNKS_UP = -(-CHUNKS // RING) * RING
A_LATENT = 0
A_MLA = A_LATENT + 4
A_SWA = A_MLA + 3 * HEADS
A_SB = A_SWA + 2 + PAIRS
A_GATE = A_SB + 3 * PAIRS
A_OUT = A_GATE + 3 * KT
A_MLP = A_OUT + KT
TILES = A_MLP + 2 * KT * GROUPS
assert TILES % 2 == 0
V_PRE, V_GATE, V_Q, V_KV, V_POST, V_MPRE, V_MPOST, V_SINK = 0, 8, 32, 34, 35, 43, 51, 59
VECS = V_SINK + HEADS
IDENT, SWAP, NEG_TRI, NEG_ONE, ONE, MASK_CAUSAL, MASK_STRICT, MASK_PREV, TRI01 = range(9)
N_CONST = 9 * P
TRIG = 4 * 5
BIG = 1e30
TWO_PI = float(2 * np.pi)
PI_PARTS = (6.28125, 0.0019340515, 1.2554228e-06, 0.0)


def pi_parts():
    left, parts = 2 * np.pi, []
    for _ in range(3):
        e = 2.0 ** (7 - np.floor(np.log2(left)))
        part = np.floor(left * e) / e
        parts.append(float(part))
        left -= part
    return parts + [float(left)]


CAUSAL = [(0, 0, 512, 0, 0), (1, 128, 384, 1, 0), (3, 384, 128, 1, 384), (2, 256, 256, 2, 0)]
BANDED = [(0, 0, 256, 0, 0), (1, 128, 256, 0, 256), (2, 256, 256, 1, 0), (3, 384, 128, 1, 256)]
CAUSAL_COLS, BANDED_COLS = 1280, 896

NORMS = [8, 2, 1, 8, 8, 8]
SQ0 = [sum(NORMS[:i]) for i in range(7)]
PRE, QLAT, KVLAT, POST, MPRE, MPOST = range(6)
H0 = {PRE: 0, QLAT: 8, KVLAT: 10, MPRE: 11}
R0 = {POST: 0, MPOST: 8}


def trunk(nc, A_x, A_pos, A_w, A_vec, A_const, A_trig, out):
    with ExitStack() as ctx:
        at = [nc.sbuf_base + (-nc.sbuf_base) % 32]

        def place(name, shape, dt, offset=None):
            size = int(np.prod(shape[1:])) * 4
            if offset is None:
                offset = at[0]
                at[0] += size + (-size) % 32
            return nc.alloc_sbuf_tensor_at(name, shape, dt, offset=offset)

        def sem(name):
            return ctx.enter_context(nc.semaphore(name))

        h_hi, h_lo = (place(n, [P, KT, SEQ], F32R) for n in ("h_hi", "h_lo"))
        x = place("x", [P, KT, SEQ], F32)
        raw = place("raw", [P, RING, CH], F32)
        w_hi, w_lo = (place(n, [P, RING, CH], F32R) for n in ("w_hi", "w_lo"))
        tab = place("tab", [P, 5, SEQ], F32)
        cst = place("cst", [P, 8, P], F32R)
        tri01 = place("tri01", [P, P], F32)
        vec_all = place("vec_all", [P, DEPTH * VECS], F32)
        vec = place("vec", [P, VECS], F32)
        trig = place("trig", [P, TRIG], F32)
        r1 = at[0]
        o_hi, o_lo = [], []
        for b in range(3):
            o_hi.append(place(f"o_hi{b}", [P, PAIRS, SEQ], F32R))
            o_lo.append(place(f"o_lo{b}", [P, PAIRS, SEQ], F32R))
        u_hi = [place("u_hi0", [P, KT, SEQ], F32R, r1)]
        u_lo = [place("u_lo0", [P, KT, SEQ], F32R, r1 + 16384)]
        y = place("y", [P, KT, SEQ], F32, r1 + 32768)
        r2 = at[0]
        at[0] += 36864
        cqn_hi = place("cqn_hi", [P, 2, SEQ], F32R, r2)
        cqn_lo = place("cqn_lo", [P, 2, SEQ], F32R, r2 + 4096)
        ckn_hi = place("ckn_hi", [P, SEQ], F32R, r2 + 8192)
        ckn_lo = place("ckn_lo", [P, SEQ], F32R, r2 + 10240)
        mq_hi = place("mq_hi", [P, 2, SEQ], F32R, r2 + 12288)
        mq_lo = place("mq_lo", [P, 2, SEQ], F32R, r2 + 16384)
        mk_hi = place("mk_hi", [P, 2, SEQ], F32R, r2 + 20480)
        mk_lo = place("mk_lo", [P, 2, SEQ], F32R, r2 + 24576)
        mv_hi = place("mv_hi", [P, 2, NB, P], F32R, r2 + 28672)
        mv_lo = place("mv_lo", [P, 2, NB, P], F32R, r2 + 32768)
        wq_hi = place("wq_hi", [P, PAIRS, SEQ], F32R, r2)
        wq_lo = place("wq_lo", [P, PAIRS, SEQ], F32R, r2 + 8192)
        wk_hi = place("wk_hi", [P, SEQ], F32R, r2 + 16384)
        wk_lo = place("wk_lo", [P, SEQ], F32R, r2 + 18432)
        wv_hi = place("wv_hi", [P, NB, 2, P], F32R, r2 + 20480)
        wv_lo = place("wv_lo", [P, NB, 2, P], F32R, r2 + 24576)
        sb_hi = [place(f"sb_hi{s}", [P, 3, SEQ], F32R, r2 + 12288 * s) for s in range(2)]
        sb_lo = [place(f"sb_lo{s}", [P, 3, SEQ], F32R, r2 + 12288 * s + 6144) for s in range(2)]
        sp_hi = place("sp_hi", [P, CAUSAL_COLS], F32R, r2 + 24576)
        sp_lo = place("sp_lo", [P, CAUSAL_COLS], F32R, r2 + 24576 + 5120)
        mix_hi = place("mix_hi", [P, KT, SEQ], F32R, r2)
        mix_lo = place("mix_lo", [P, KT, SEQ], F32R, r2 + 16384)
        u_hi.append(place("u_hi1", [P, KT, SEQ], F32R, r2))
        u_lo.append(place("u_lo1", [P, KT, SEQ], F32R, r2 + 16384))
        cst_f = place("cst_f", [P, N_CONST], F32, r2)
        pos_i = place("pos_i", [P, SEQ], I32, r2 + 8192)
        r3 = at[0]
        at[0] += 24576
        s_f = place("s_f", [P, CAUSAL_COLS], F32, r3)
        p_hi = place("p_hi", [P, CAUSAL_COLS], F32R, r3 + 5120)
        p_lo = place("p_lo", [P, CAUSAL_COLS], F32R, r3 + 10240)
        fb = [place("fb0", [P, CAUSAL_COLS], F32, r3), place("fb1", [P, CAUSAL_COLS], F32, r3 + 15360)]
        mx = place("mx", [P, SEQ], F32, r3 + 15360)
        mxr = place("mxr", [P, SEQ], F32, r3 + 17408)
        bs_f = place("bs_f", [P, BANDED_COLS], F32, r3)
        bp_hi = place("bp_hi", [P, BANDED_COLS], F32R, r3 + 3584)
        bp_lo = place("bp_lo", [P, BANDED_COLS], F32R, r3 + 7168)
        bmx = [place(f"bmx{s}", [P, SEQ], F32, r3 + 10752 + 2048 * s) for s in range(2)]
        bmxr = [place(f"bmxr{s}", [P, SEQ], F32, r3 + 14848 + 2048 * s) for s in range(2)]
        of = place("of", [P, SEQ], F32, r3 + 20480)
        dn = place("dn", [P, SEQ], F32, r3 + 22528)
        sq = place("sq", [P, 2, SEQ], F32, r3)
        acc = place("acc", [P, SEQ], F32, r3 + 4096)
        acc_hi = place("acc_hi", [P, SEQ], F32R, r3 + 6144)
        acc_lo = place("acc_lo", [P, SEQ], F32R, r3 + 8192)
        ms = place("ms", [P, SEQ], F32, r3 + 10240)
        rs0 = place("rs0", [P, SEQ], F32, r3 + 12288)
        rst = place("rst", [P, SEQ], F32, r3 + 14336)
        rstd = place("rstd", [P, SEQ], F32, r3 + 16384)
        hf = place("hf", [P, 2, SEQ], F32, r3 + 18432)
        gate = place("gate", [P, 2, SEQ], F32, r3)
        prod = place("prod", [P, SEQ], F32, r3 + 4096)
        mix = place("mix", [P, 2, SEQ], F32, r3 + 6144)
        relu = place("relu", [P, 2, SEQ], F32, r3)
        usq = place("usq", [P, 2, SEQ], F32, r3 + 4096)
        cf = place("cf", [P, 3, SEQ], F32, r1 + 16384)
        ra = place("ra", [P, SEQ], F32, r1 + 16384 + 6144)
        rb = place("rb", [P, SEQ], F32, r1 + 16384 + 8192)
        rp_hi = place("rp_hi", [P, SEQ], F32R, r1 + 16384 + 10240)
        rp_lo = place("rp_lo", [P, SEQ], F32R, r1 + 16384 + 12288)
        tables = [place(f"tt{i}", [P, SEQ], F32, r3 + 2048 * i) for i in range(4)]
        COS, SIN, QPE, KCOS, KSIN = (tab[:, i, :] for i in range(5))
        mqf = place("mqf", [P, SEQ], F32, r1 + 32768)
        assert at[0] <= nc.sbuf_usable_end if hasattr(nc, "sbuf_usable_end") else True

        bank = [ctx.enter_context(nc.psum_tensor(f"bank{i}", [P, SEQ], F32)) for i in range(8)]
        proj, score = bank[0:2], bank[2:5]
        merge_bank = bank[2:4]
        pv_bank, rot_bank, norm_bank = bank[5], bank[6], bank[7]
        band = [[bank[2], bank[3]], [bank[4], bank[6]]]
        stick = [[(bank[2], 0), (bank[3], 0), (bank[4], 0)], [(bank[6], 0), (bank[7], 0), (bank[4], 256)]]
        STICK_COLS = (512, 512, 256)

        small_loaded = sem("small_loaded")
        stored = sem("stored")
        setup_act, setup_dve = sem("setup_act"), sem("setup_dve")
        cleared = []

        def signal(name, per_layer):
            cleared.append(sem(name))
            return cleared[-1]

        loaded = [signal(f"loaded{s}", 0) for s in range(RING)]
        whi = signal("w_hi_ready", CHUNKS)
        wlo = signal("w_lo_ready", CHUNKS)
        vec_set = signal("vec_set", 1)
        ones_set = signal("ones_set", 4)
        full = signal("tile_full", TILES)
        free = [signal(f"tile_free{b}", TILES // 2) for b in range(2)]
        squared = signal("squared", SQ0[6])
        summed = signal("summed", SQ0[6])
        sum_split = signal("sum_split", 12)
        sum_all = signal("sum_all", 6)
        rs_guess = signal("rs_guess", 12)
        rs_step = signal("rs_step", 24)
        hf_set = signal("hf_set", 19)
        hhi = signal("h_hi_ready", 19)
        hlo = signal("h_lo_ready", 19)
        res = signal("residual", 32)
        kr_part = signal("kr_part", 1)
        kr_sum = signal("kr_sum", 1)
        kr_hi = signal("kr_hi", 2)
        kr_lo = signal("kr_lo", 2)
        mq_f = signal("mla_q_f", HEADS)
        mq_h = signal("mla_q_hi", HEADS)
        mq_l = signal("mla_q_lo", HEADS)
        mk_h = signal("mla_k_hi", HEADS)
        mv_h = signal("mla_v_hi", HEADS)
        rp_h = signal("rope_in_hi", 5)
        rp_l = signal("rope_in_lo", 5)
        rot = signal("rotated", 5)
        rot_used = signal("rot_used", 5)
        rp_sum = signal("rope_sum", 5)
        rpo_h = signal("rope_out_hi", 5)
        rpo_l = signal("rope_out_lo", 5)
        wv_h = signal("swa_v_hi", 1)
        sbh = signal("sb_in_hi", 3 * PAIRS)
        score_full = signal("score_full", 3 * HEADS + 2 * HEADS + 3 * HEADS)
        shared_half = signal("shared_half", PAIRS)
        score_free = signal("score_free", 2 * HEADS)
        mx_step = signal("max_step", 8 * HEADS)
        mx_all = signal("max_all", 2 * HEADS)
        mx_sink = signal("max_sink", HEADS)
        sub = signal("subtracted", 2 * HEADS)
        p_exp = signal("p_exp", 2 * HEADS)
        p_h = signal("p_hi_ready", 3 * HEADS)
        p_l = signal("p_lo_ready", 3 * HEADS)
        pv_full = signal("pv_full", 3 * HEADS)
        pv_free = signal("pv_free", 3 * HEADS)
        sink_e = signal("sink_exp", HEADS)
        den = signal("denominator", HEADS)
        den_inv = signal("den_inv", 4 * HEADS)
        o_h = signal("o_hi_ready", 2 * PAIRS)
        o_l = signal("o_lo_ready", 2 * PAIRS)
        z_min = signal("z_min", 3 * HEADS)
        z_exp = signal("z_exp", HEADS)
        z_ln = signal("z_ln", HEADS)
        z_max = signal("z_max", 3 * HEADS)
        z_mask = signal("z_mask", 4 * HEADS)
        sp_h = signal("sp_hi_ready", HEADS)
        sp_l = signal("sp_lo_ready", HEADS)
        tail_full = signal("tail_full", 3 * HEADS)
        a_exp = signal("a_exp", 3 * HEADS)
        sbo_h = signal("sb_o_hi", HEADS)
        merge_full = signal("merge_full", 3 * KT)
        merge_free = [signal(f"merge_free{b}", 3 * KT // 2) for b in range(2)]
        mix_add = signal("mix_add", 2 * KT)
        mix_h = signal("mix_hi_ready", KT)
        mix_l = signal("mix_lo_ready", KT)
        u_h = signal("u_hi_ready", KT * GROUPS)
        u_s = signal("u_squared", KT * GROUPS)
        u_l = signal("u_lo_ready", KT * GROUPS)

        MLP = [("up", 0)]
        for g in range(GROUPS):
            if g + 1 < GROUPS:
                MLP.append(("up", g + 1))
            MLP.append(("down", g))

        def merge_plan():
            for u in range(KT // 2):
                for b in range(3):
                    c = C_MERGE + 9 * u + 3 * b
                    n = 6 * u + 2 * b
                    yield "gate", b, 2 * u, c, 0, n
                    yield "o", b, 2 * u, c + 1, 0, n
                    yield "o", b, 2 * u + 1, c + 1, 1, n + 1
                    yield "gate", b, 2 * u + 1, c + 2, 0, n + 1

        with nc.Block() as block:

            @block.sync
            def _(sp):
                sp.dma_start(cst_f[:, :], A_const).then_inc(small_loaded, 16)
                sp.dma_start(trig[:, :], A_trig).then_inc(small_loaded, 16)
                sp.dma_start(vec_all[:, :], A_vec).then_inc(small_loaded, 16)
                sp.dma_start(pos_i[:, :], A_pos.broadcast_to([P, SEQ])).then_inc(small_loaded, 16)
                sp.dma_start(x[:, :, :], A_x).then_inc(small_loaded, 16)

            @block.scalar
            def _(act):
                for i in range(5):
                    act.wait_ge(setup_dve, 10 * (i + 1))
                    act.activation(tab[:, i, :], tables[0][:, :], ACT.Sin).then_inc(setup_act, 1)

            @block.vector
            def _(dve):
                steps = [0]

                def step(ins):
                    steps[0] += 1
                    ins.then_inc(setup_dve, 1)
                    dve.wait_ge(setup_dve, steps[0])

                dve.wait_ge(small_loaded, 5 * 16)
                parts = pi_parts()
                for i in range(5):
                    ang, turns = tables[0], tables[1]
                    col = lambda j: trig[:, 4 * i + j:4 * i + j + 1]
                    if i:
                        dve.wait_ge(setup_act, i)
                    step(dve.tensor_copy(tables[2][:, :], pos_i[:, :]))
                    step(dve.tensor_scalar(ang[:, :], tables[2][:, :], col(0), None, ALU.mult))
                    step(dve.tensor_scalar(turns[:, :], ang[:, :], 1.0 / TWO_PI, col(1), ALU.mult, ALU.add))
                    step(dve.tensor_scalar(turns[:, :], turns[:, :], 12582912.0, -12582912.0, ALU.add, ALU.add))
                    for part in parts[:3]:
                        step(dve.scalar_tensor_tensor(out=ang[:, :], in0=turns[:, :], scalar=-part, in1=ang[:, :],
                                                      op0=ALU.mult, op1=ALU.add))
                    step(dve.scalar_tensor_tensor(out=ang[:, :], in0=turns[:, :], scalar=-parts[3], in1=ang[:, :],
                                                  op0=ALU.mult, op1=ALU.add))
                    step(dve.tensor_scalar(ang[:, :], ang[:, :], col(2), 3.1415925, ALU.add, ALU.min))
                    step(dve.tensor_scalar(ang[:, :], ang[:, :], -3.1415925, None, ALU.max))
                dve.wait_ge(setup_act, 5)
                for i in (1, 2, 4):
                    step(dve.tensor_scalar(tab[:, i, :], tab[:, i, :], trig[:, 4 * i + 3:4 * i + 4], None, ALU.mult))
                step(dve.memset(tab[0:HEAD, 2, :], 1.0))
                step(dve.tensor_copy(tri01[:, :], cst_f[:, TRI01 * P:(TRI01 + 1) * P]))
                step(dve.tensor_copy(cst[:, :, :], cst_f[:, 0:8 * P].rearrange("p (a c) -> p a c", a=8)))

        def used(c):
            if c < C_MLA:
                return full, A_LATENT + c + 1
            if c < C_SWA:
                return full, A_MLA + 6 * (c - C_MLA) + 6
            if c < C_MERGE:
                return full, A_SWA + c - C_SWA + 1
            if c < C_OUT:
                return max(((merge_full, n + 1) if kind == "o" else (full, A_GATE + n + 1)
                            for kind, b, t, cc, i, n in merge_plan() if cc == c), key=lambda s: s[1])
            return full, A_OUT + c - C_OUT + 1

        with nc.Fori(0, DEPTH) as l:
            with nc.Block() as block:
                @block.sync
                def _(sp):
                    for c in range(CHUNKS):
                        if c >= RING:
                            sp.wait_ge(wlo, c + 1 - RING)
                        sp.dma_start(raw[:, c % RING, :], A_w[l, c]).then_inc(loaded[c % RING], 16)

                @block.tensor
                def _(pe):

                    def three(o, pairs, start=True, last=True, mm=None):
                        n = len(pairs)
                        for i, ((a, al), (b, bl)) in enumerate(pairs):
                            for j, (s, m) in enumerate(((a, b), (a, bl), (al, b))):
                                mm = pe.matmul(o, s, m, start=start and i == 0 and j == 0,
                                               stop=last and i == n - 1 and j == 2, skip_group_check=True)
                        return mm

                    def add(o, stationary, moving):
                        return pe.matmul(o, stationary, moving, start=False, stop=True, skip_group_check=True)

                    def norm_sum(nu):
                        pe.wait_ge(sum_split, 2 * nu + 2)
                        if nu:
                            pe.wait_ge(rs_step, 4 * (nu - 1) + 1)
                        pe.matmul(norm_bank[:, :], cst[:, ONE, :], acc_hi[:, :], start=True, stop=False)
                        pe.matmul(norm_bank[:, :], cst[:, ONE, :], acc_lo[:, :], start=False, stop=True)\
                          .then_inc(sum_all, 1)

                    def take_bank(k):
                        if k > 1:
                            pe.wait_ge(free[k % 2], k // 2)

                    def weight(c, i):
                        return (w_hi[:, c % RING, i * P:(i + 1) * P], w_lo[:, c % RING, i * P:(i + 1) * P])

                    def tile(c, k, hi, lo, ready=None):
                        pe.wait_ge(wlo, c + 1)
                        take_bank(k)
                        for t in range(KT):
                            if ready:
                                pe.wait_ge(ready[0], ready[1] + t + 1)
                            mm = three(proj[k % 2][:, :], [(weight(c, t), (hi[:, t, :], lo[:, t, :]))],
                                       start=t == 0, last=t == KT - 1)
                        mm.then_inc(full, 1)

                    def value_tile(c, k):
                        pe.wait_ge(wlo, c + 1)
                        take_bank(k)
                        for j in range(NB):
                            tok = slice(j * P, (j + 1) * P)
                            mm = three(proj[k % 2][:, tok],
                                       [((h_hi[:, t, tok], h_lo[:, t, tok]), weight(c, t)) for t in range(KT)],
                                       start=j == 0)
                        mm.then_inc(full, 1)

                    def scores(pieces, banks, keys, queries, masks):
                        for n, (j, q0, w, b, col) in enumerate(pieces):
                            to, off = banks[b]
                            mm = three(to[:, off + col:off + col + w], [(keys(j), queries(q0, w))],
                                       start=off + col == 0)
                            for i, m in enumerate(masks[:w // P]):
                                mm = add(to[:, off + col + i * P:off + col + (i + 1) * P], cst[:, m, :],
                                         cst[:, IDENT, :])
                            if n + 1 == len(pieces) or pieces[n + 1][3] != b:
                                mm.then_inc(score_full, 1)

                    def values(n, pieces, cols, vals):
                        pe.wait_ge(p_l, n + 1)
                        if n:
                            pe.wait_ge(pv_free, n)
                        for i, (j, q0, w, b, col) in enumerate(pieces):
                            if pieces is BANDED:
                                s = slice(q0 * 2, q0 * 2 + w)
                                probs = bp_hi[:, s], bp_lo[:, s]
                            else:
                                s = slice(b * SEQ + col, b * SEQ + col + w)
                                probs = p_hi[:, s], p_lo[:, s]
                            mm = three(pv_bank[:, q0:q0 + w], [(vals(j), probs)], start=i == 0)
                        mm.then_inc(pv_full, 1)

                    norm_sum(PRE)
                    for i in range(4):
                        tile(C_LATENT + i, A_LATENT + i, h_hi, h_lo, (hlo, 0) if i == 0 else None)
                    norm_sum(QLAT)
                    norm_sum(KVLAT)

                    def mla_qk(h):
                        c, k, w0 = C_MLA + h // 2, A_MLA + 3 * h, 3 * (h % 2)
                        pe.wait_ge(wlo, c + 1)
                        pe.wait_ge(hlo, 11)
                        take_bank(k)
                        three(proj[k % 2][:, :], [(weight(c, w0 + t), (cqn_hi[:, t, :], cqn_lo[:, t, :]))
                                                  for t in range(2)]).then_inc(full, 1)
                        take_bank(k + 1)
                        three(proj[(k + 1) % 2][:, :], [(weight(c, w0 + 2), (ckn_hi[:, :], ckn_lo[:, :]))])\
                            .then_inc(full, 1)

                    def mla_v(h):
                        c, k, w0 = C_MLA + h // 2, A_MLA + 3 * h + 2, 3 * (h % 2)
                        take_bank(k)
                        whi_, wlo_ = weight(c, w0 + 2)
                        for j in range(NB):
                            tok = slice(j * P, (j + 1) * P)
                            mm = three(proj[k % 2][:, j * HEAD:(j + 1) * HEAD],
                                       [((ckn_hi[:, tok], ckn_lo[:, tok]), (whi_[:, HEAD:P], wlo_[:, HEAD:P]))],
                                       start=j == 0)
                        mm.then_inc(full, 1)

                    def mla_scores(h):
                        s = h % 2
                        pe.wait_ge(mq_l, h + 1)
                        k = A_MLA + 3 * h + 1
                        pe.wait_ge(free[k % 2], k // 2 + 1)
                        if h == 0:
                            pe.wait_ge(kr_lo, 2)
                        else:
                            pe.wait_ge(score_free, h)
                        scores(CAUSAL, [(b, 0) for b in score],
                               lambda j: (mk_hi[:, s, j * P:(j + 1) * P], mk_lo[:, s, j * P:(j + 1) * P]),
                               lambda q0, w: (mq_hi[:, s, q0:q0 + w], mq_lo[:, s, q0:q0 + w]), [MASK_CAUSAL])

                    def mla_values(h):
                        s = h % 2
                        k = A_MLA + 3 * h + 2
                        pe.wait_ge(free[k % 2], k // 2 + 1)
                        if h == 0:
                            pe.wait_ge(ones_set, 2)
                        values(h, CAUSAL, CAUSAL_COLS, lambda j: (mv_hi[:, s, j, :], mv_lo[:, s, j, :]))

                    mla_qk(0)
                    mla_v(0)
                    mla_scores(0)
                    mla_qk(1)
                    mla_v(1)
                    for h in range(HEADS):
                        if h + 1 < HEADS:
                            mla_scores(h + 1)
                        if h + 2 < HEADS:
                            mla_qk(h + 2)
                        mla_values(h)
                        if h + 2 < HEADS:
                            mla_v(h + 2)

                    def rotate(n):
                        pe.wait_ge(rp_l, n + 1)
                        if n:
                            pe.wait_ge(rot_used, n)
                        pe.matmul(rot_bank[:, :], cst[:, SWAP, :], rp_hi[:, :], start=True, stop=False)
                        pe.matmul(rot_bank[:, :], cst[:, SWAP, :], rp_lo[:, :], start=False, stop=True)\
                          .then_inc(rot, 1)

                    tile(C_SWA, A_SWA, h_hi, h_lo)
                    value_tile(C_SWA + 1, A_SWA + 1)
                    rotate(0)
                    for t in range(PAIRS):
                        tile(C_SWA + 2 + t, A_SWA + 2 + t, h_hi, h_lo)
                        if t:
                            rotate(t)
                    rotate(PAIRS)
                    def band_scores(n):
                        t, r = n // 2, n % 2
                        rows = slice(HEAD * r, HEAD * (r + 1))
                        pe.wait_ge(rpo_l, t + 2)
                        pe.wait_ge(rot_used, PAIRS + 1)
                        pe.wait_ge(score_free, HEADS + max(n - 1, 0))
                        scores(BANDED, [(b, 0) for b in band[r]],
                               lambda j: (wk_hi[rows, j * P:(j + 1) * P], wk_lo[rows, j * P:(j + 1) * P]),
                               lambda q0, w: (wq_hi[rows, t, q0:q0 + w], wq_lo[rows, t, q0:q0 + w]),
                               [MASK_CAUSAL, MASK_PREV])

                    k = A_SWA + 1
                    pe.wait_ge(free[k % 2], k // 2 + 1)
                    pe.wait_ge(ones_set, 4)
                    band_scores(0)
                    band_scores(1)
                    for n in range(HEADS):
                        if n + 2 < HEADS:
                            band_scores(n + 2)
                        values(HEADS + n, BANDED, BANDED_COLS, lambda j: (wv_hi[:, j, n % 2, :], wv_lo[:, j, n % 2, :]))

                    def stick_scores(p):
                        for i in range(2):
                            k = A_SB + 3 * p + i
                            pe.wait_ge(free[k % 2], k // 2 + 1)
                        if p:
                            pe.wait_ge(a_exp, 6 * p)
                        else:
                            pe.wait_ge(score_free, 2 * HEADS)
                        s = p % 2

                        def piece(r, n):
                            j, q0, w, b, col = CAUSAL[n]
                            rows = slice(HEAD * r, HEAD * (r + 1))
                            to, off = stick[r][b]
                            key, query = slice(j * P, (j + 1) * P), slice(q0, q0 + w)
                            return three(to[:, off + col:off + col + w],
                                         [((sb_hi[s][rows, 1, key], sb_lo[s][rows, 1, key]),
                                           (sb_hi[s][rows, 0, query], sb_lo[s][rows, 0, query]))],
                                         start=off + col == 0)

                        piece(0, 0).then_inc(score_full, 1)
                        piece(0, 1)
                        piece(0, 2).then_inc(score_full, 1)
                        piece(0, 3).then_inc(shared_half, 1)
                        pe.wait_ge(shared_half, p + 1)
                        piece(1, 3).then_inc(score_full, 1)
                        piece(1, 0).then_inc(score_full, 1)
                        piece(1, 1)
                        piece(1, 2).then_inc(score_full, 1)

                    def stick_tail(h):
                        pe.wait_ge(sp_l, h + 1)
                        for n, (j, q0, w, b, col) in enumerate(CAUSAL):
                            to, off = stick[h % 2][b]
                            if h % 2 and b == 2:
                                pe.wait_ge(a_exp, 3 * h)
                            for (j2, q2, w2, b2, col2) in CAUSAL:
                                if j2 < j:
                                    continue
                                m = NEG_TRI if j2 == j else NEG_ONE
                                o = to[:, off + col + q2 - q0:off + col + w]
                                s = slice(b2 * SEQ + col2, b2 * SEQ + col2 + w2)
                                add(o, cst[:, m, :], sp_hi[:, s])
                                add(o, cst[:, m, :], sp_lo[:, s])
                            mm = add(to[:, off + col:off + col + P], cst[:, MASK_STRICT, :], cst[:, IDENT, :])
                            if n != 1:
                                mm.then_inc(tail_full, 1)

                    def stick_values(h):
                        s, k = h // 2 % 2, A_SB + 3 * (h // 2) + 2
                        pe.wait_ge(free[k % 2], k // 2 + 1)
                        values(2 * HEADS + h, CAUSAL, CAUSAL_COLS,
                               lambda j: (sb_hi[s][:, 2, j * P:(j + 1) * P], sb_lo[s][:, 2, j * P:(j + 1) * P]))

                    tile(C_SB, A_SB, h_hi, h_lo)
                    tile(C_SB + 1, A_SB + 1, h_hi, h_lo)
                    value_tile(C_SB + 2, A_SB + 2)
                    stick_scores(0)
                    for p in range(PAIRS):
                        c, k = C_SB + 3 * (p + 1), A_SB + 3 * (p + 1)
                        if p + 1 < PAIRS:
                            tile(c, k, h_hi, h_lo)
                            tile(c + 1, k + 1, h_hi, h_lo)
                        stick_tail(2 * p)
                        stick_tail(2 * p + 1)
                        if p + 1 < PAIRS:
                            value_tile(c + 2, k + 2)
                        stick_values(2 * p)
                        if p + 1 < PAIRS:
                            stick_scores(p + 1)
                        stick_values(2 * p + 1)

                    pe.wait_ge(a_exp, 3 * HEADS)
                    for b in range(2):
                        pe.wait_ge(o_l, 2 * PAIRS)
                    pe.wait_ge(pv_free, 3 * HEADS)
                    for kind, b, t, c, i, n in merge_plan():
                        if kind == "gate":
                            tile(c, A_GATE + n, h_hi, h_lo)
                            continue
                        pe.wait_ge(wlo, c + 1)
                        if n > 1:
                            pe.wait_ge(merge_free[n % 2], n // 2)
                        three(merge_bank[n % 2][:, :], [(weight(c, 4 * i + q), (o_hi[b][:, q, :], o_lo[b][:, q, :]))
                                                        for q in range(PAIRS)]).then_inc(merge_full, 1)

                    for t in range(KT):
                        tile(C_OUT + t, A_OUT + t, mix_hi, mix_lo, (mix_l, 0) if t == 0 else None)
                    norm_sum(POST)
                    norm_sum(MPRE)

                    k = 0
                    for what, g in MLP:
                        for t in range(KT):
                            if what == "up":
                                tile(C_MLP + k, A_MLP + k, h_hi, h_lo, (hlo, H0[MPRE]) if k == 0 else None)
                            else:
                                tile(C_MLP + k, A_MLP + k, u_hi[g % 2], u_lo[g % 2],
                                     (u_l, KT * g) if t == 0 else None)
                            k += 1
                    norm_sum(MPOST)

                @block.scalar
                def _(act):
                    LN_EXP = "natural_log_exp_and_others"

                    def split(c):
                        if c >= CHUNKS:
                            return
                        n = c // RING + 1
                        act.wait_ge(loaded[c % RING], 16 * (c // RING + 1))
                        if c >= RING:
                            act.wait_ge(*used(c - RING))
                        act.activation(w_hi[:, c % RING, :], raw[:, c % RING, :], ACT.Copy).then_inc(whi, 1)

                    def square(n, src, after=None):
                        if after:
                            act.wait_ge(after[0], after[1])
                        if n > 1:
                            act.wait_ge(summed, n - 1)
                        act.activation(sq[:, n % 2, :], src, ACT.Square).then_inc(squared, 1)

                    def norm_guess(nu, width):
                        act.wait_ge(sum_all, nu + 1)
                        act.activation(rs0[:, :], norm_bank[:, :], ACT.Ln, bias=EPS, scale=1.0 / width)\
                           .then_inc(rs_guess, 1)
                        act.wait_ge(rs_guess, 2 * nu + 1)
                        act.activation(rs0[:, :], rs0[:, :], ACT.Exp, scale=-0.5).then_inc(rs_guess, 1)

                    def norm_hi(nu, n, dst):
                        act.wait_ge(hf_set, n + 1)
                        act.activation(dst, hf[:, n % 2, :], ACT.Copy).then_inc(hhi, 1)

                    def tile_ready(k):
                        act.wait_ge(full, k + 1)

                    def soft_out(n):
                        if n < HEADS:
                            act.wait_ge(pv_full, n + 1)
                            src = pv_bank[HEAD:P, :]
                        else:
                            act.wait_ge(den, n - HEADS + 1)
                            src = dn[HEAD:P, :]
                        if n > 0:
                            act.wait_ge(pv_free, n)
                        act.activation(dn[0:HEAD, :], src, ACT.Ln).then_inc(den_inv, 1)
                        act.wait_ge(den_inv, 2 * n + 1)
                        act.activation(dn[0:HEAD, :], dn[0:HEAD, :], ACT.Exp, scale=-1.0).then_inc(den_inv, 1)

                    def out_hi(n):
                        b, q = n // 2 // PAIRS, n // 2 % PAIRS
                        act.wait_ge(pv_free, n + 1)
                        act.activation(o_hi[b][:, q, :], of[:, :], ACT.Copy).then_inc(o_h, 1)

                    def soft_exp(n, src, dst, scale):
                        act.wait_ge(sub, n + 1)
                        act.activation(src, src, ACT.Exp, scale=scale).then_inc(p_exp, 1)
                        act.wait_ge(p_exp, n + 1)
                        if n > 0:
                            act.wait_ge(pv_full, n)
                        act.activation(dst, src, ACT.Copy).then_inc(p_h, 1)

                    act.preload_act_table_set(LN_EXP)
                    for t in range(KT):
                        square(t, x[:, t, :])
                    split(0)
                    split(1)
                    norm_guess(PRE, D)
                    for t in range(KT):
                        norm_hi(PRE, t, h_hi[:, t, :])
                    for i in range(4):
                        split(C_LATENT + i + 2)
                        tile_ready(i)
                        if i < 3:
                            act.activation(cf[:, i, :], proj[i % 2][:, :], ACT.Copy).then_inc(free[i % 2], 1)
                    for i in range(3):
                        k = i
                        square(SQ0[QLAT] + i, cf[:, i, :], (free[i % 2], i // 2 + 1))
                    norm_guess(QLAT, Q_LORA)
                    for i in range(2):
                        norm_hi(QLAT, 8 + i, cqn_hi[:, i, :])
                    norm_guess(KVLAT, KV_LORA)
                    norm_hi(KVLAT, 10, ckn_hi[:, :])
                    for s in range(2):
                        act.wait_ge(kr_sum, 1)
                        act.activation(mk_hi[HEAD:P, s, :], ra[HEAD:P, :], ACT.Copy).then_inc(kr_hi, 1)

                    def mla_qk(h):
                        k, s = A_MLA + 3 * h, h % 2
                        if h % 2 == 0:
                            split(C_MLA + h // 2 + 2)
                        act.wait_ge(mq_f, h + 1)
                        act.activation(mq_hi[:, s, :], mqf[:, :], ACT.Copy).then_inc(mq_h, 1)
                        tile_ready(k + 1)
                        act.activation(mk_hi[0:HEAD, s, :], proj[(k + 1) % 2][0:HEAD, :], ACT.Copy)\
                           .then_inc(mk_h, 1)

                    def mla_v(h):
                        k, s = A_MLA + 3 * h + 2, h % 2
                        tile_ready(k)
                        act.activation(mv_hi[:, s, :, 0:HEAD],
                                       proj[k % 2][:, 0:NB * HEAD].rearrange("p (j d) -> p j d", j=NB), ACT.Copy)\
                           .then_inc(mv_h, 1)

                    for h in range(2):
                        mla_qk(h)
                        mla_v(h)
                    for h in range(HEADS):
                        soft_exp(h, s_f[:, :], p_hi[:, :], float((HEAD + ROPE_DIM) ** -0.5))
                        if h + 2 < HEADS:
                            mla_qk(h + 2)
                        soft_out(h)
                        if h + 2 < HEADS:
                            mla_v(h + 2)
                        if h % 2:
                            out_hi(h)

                    def rope(n, k, scale, dst):
                        tile_ready(k)
                        if n:
                            act.wait_ge(rot, n)
                        act.activation(rp_hi[:, :], proj[k % 2][:, :], ACT.Copy, scale=scale).then_inc(rp_h, 1)

                    def rope_out(n, dst):
                        act.wait_ge(rp_sum, n + 1)
                        act.activation(dst, ra[:, :], ACT.Copy).then_inc(rpo_h, 1)

                    split(C_SWA + 2)
                    rope(0, A_SWA, 1.0, None)
                    rope_out(0, wk_hi[:, :])
                    split(C_SWA + 3)
                    tile_ready(A_SWA + 1)
                    act.activation(wv_hi[:, :, :, 0:HEAD],
                                   proj[(A_SWA + 1) % 2][:, :].rearrange("p (j v d) -> p j v d", j=NB, v=2), ACT.Copy)\
                       .then_inc(wv_h, 1)
                    for t in range(PAIRS):
                        split(C_SWA + 4 + t)
                        rope(t + 1, A_SWA + 2 + t, 0.125, None)
                        rope_out(t + 1, wq_hi[:, t, :])
                    for n in range(HEADS + 1):
                        if n < HEADS:
                            soft_exp(HEADS + n, bs_f[:, :], bp_hi[:, :], 1.0)
                        if n:
                            soft_out(HEADS + n - 1)
                        if n < HEADS:
                            head = n // 2 + 4 * (n % 2)
                            act.wait_ge(mx_sink, n + 1)
                            act.wait_ge(den_inv, 2 * (HEADS + n) - 1)
                            act.activation(dn[HEAD:P, :], bmxr[n % 2][HEAD:P, :], ACT.Exp, scale=-1.0,
                                           bias=vec[HEAD:P, V_SINK + head:V_SINK + head + 1]).then_inc(sink_e, 1)
                        if n and n % 2 == 0:
                            out_hi(HEADS + n - 1)

                    def stick_in(p, i):
                        c, k = C_SB + 3 * p + i, A_SB + 3 * p + i
                        split(c + 2)
                        tile_ready(k)
                        act.activation(sb_hi[p % 2][:, i, :], proj[k % 2][:, :], ACT.Copy, scale=0.125 if i == 0 else 1.0)\
                           .then_inc(sbh, 1)

                    def stick_ln(h):
                        b = fb[h % 2][:, :]
                        act.wait_ge(z_exp, h + 1)
                        act.activation(b, b, ACT.Ln, bias=1.0).then_inc(z_ln, 1)

                    def stick_exp(h):
                        b = fb[h % 2][:, :]
                        act.wait_ge(z_min, 3 * h + 3)
                        act.activation(b, b, ACT.Exp).then_inc(z_exp, 1)

                    def stick_hi(h):
                        act.wait_ge(z_mask, 4 * h + 4)
                        if h > 0:
                            act.wait_ge(tail_full, 3 * h)
                        act.activation(sp_hi[:, :], fb[h % 2][:, :], ACT.Copy).then_inc(sp_h, 1)

                    def stick_probs(h):
                        act.wait_ge(sp_l, h + 1)
                        for b, w in enumerate(STICK_COLS):
                            act.wait_ge(tail_full, 3 * h + b + 1)
                            src, off = stick[h % 2][b]
                            act.activation(fb[h % 2][:, b * SEQ:b * SEQ + w], src[:, off:off + w], ACT.Exp)\
                               .then_inc(a_exp, 1)

                    def stick_probs_hi(h):
                        act.wait_ge(a_exp, 3 * h + 3)
                        act.wait_ge(pv_full, 2 * HEADS + h)
                        act.activation(p_hi[:, :], fb[h % 2][:, :], ACT.Copy).then_inc(p_h, 1)

                    def stick_out(h):
                        rows = slice(HEAD * (h % 2), HEAD * (h % 2 + 1))
                        act.wait_ge(pv_full, 2 * HEADS + h + 1)
                        act.activation(o_hi[2][rows, h // 2, :], pv_bank[rows, :], ACT.Copy).then_inc(sbo_h, 1)

                    for i in range(3):
                        stick_in(0, i)
                    for p in range(PAIRS):
                        h, more = 2 * p, p + 1 < PAIRS
                        stick_exp(h)
                        stick_ln(h)
                        stick_exp(h + 1)
                        stick_ln(h + 1)
                        if p:
                            stick_out(h - 1)
                        if more:
                            stick_in(p + 1, 0)
                        stick_hi(h)
                        if more:
                            stick_in(p + 1, 1)
                        stick_hi(h + 1)
                        stick_probs(h)
                        stick_probs_hi(h)
                        stick_probs(h + 1)
                        if more:
                            stick_in(p + 1, 2)
                        stick_out(h)
                        stick_probs_hi(h + 1)
                    stick_out(HEADS - 1)

                    for kind, b, t, c, i, n in merge_plan():
                        if i == 0:
                            split(c + 2)
                        if kind == "gate":
                            k = A_GATE + n
                            tile_ready(k)
                            if n > 1:
                                act.wait_ge(merge_free[n % 2], n // 2)
                            act.activation(gate[:, n % 2, :], proj[k % 2][:, :], ACT.Sigmoid,
                                           bias=vec[:, V_GATE + KT * b + t:V_GATE + KT * b + t + 1])\
                               .then_inc(free[k % 2], 1)
                        if kind == "gate" and b == 2 and t % 2:
                            for t2 in (t - 1, t):
                                act.wait_ge(mix_add, 4 * (t // 2) + 3 + t2 % 2)
                                act.activation(mix_hi[:, t2, :], mix[:, t2 % 2, :], ACT.Copy).then_inc(mix_h, 1)
                    act.preload_act_table_set(LN_EXP)

                    for t in range(KT):
                        k = A_OUT + t
                        split(C_OUT + t + 2)
                        tile_ready(k)
                        act.activation(y[:, t, :], proj[k % 2][:, :], ACT.Copy).then_inc(free[k % 2], 1)
                        square(SQ0[POST] + t, y[:, t, :], (free[k % 2], k // 2 + 1))
                    norm_guess(POST, D)
                    for t in range(KT):
                        square(SQ0[MPRE] + t, x[:, t, :], (res, 2 * t + 2))
                    norm_guess(MPRE, D)
                    for t in range(KT):
                        norm_hi(MPRE, H0[MPRE] + t, h_hi[:, t, :])

                    k = 0
                    for what, g in MLP:
                        for t in range(KT):
                            kk = A_MLP + k
                            split(C_MLP + k + 2)
                            if what == "up":
                                n = KT * g + t
                                tile_ready(kk)
                                if n > 1:
                                    act.wait_ge(u_s, n - 1)
                                if n > 1:
                                    act.wait_ge(u_h, n - 1)
                                act.activation(relu[:, n % 2, :], proj[kk % 2][:, :], ACT.Relu)\
                                   .then_inc(free[kk % 2], 1)
                                act.wait_ge(free[kk % 2], kk // 2 + 1)
                                act.activation(u_hi[g % 2][:, t, :], relu[:, n % 2, :], ACT.Square)\
                                   .then_inc(u_h, 1)
                            elif g == GROUPS - 1:
                                square(SQ0[MPOST] + t, y[:, t, :], (free[kk % 2], kk // 2 + 1))
                            k += 1
                    norm_guess(MPOST, D)

                @block.vector
                def _(dve):
                    def split(c):
                        if c >= CHUNKS:
                            return
                        dve.wait_ge(whi, c + 1)
                        dve.tensor_tensor(w_lo[:, c % RING, :], raw[:, c % RING, :], w_hi[:, c % RING, :].bitcast(F32),
                                          ALU.subtract).then_inc(wlo, 1)

                    def gather(nu, first_tile, tiles, n0):
                        for i in range(tiles):
                            n = n0 + i
                            dve.wait_ge(squared, n + 1)
                            if i == 0:
                                if nu:
                                    dve.wait_ge(sum_split, 2 * nu)
                                dve.tensor_copy(acc[:, :], sq[:, n % 2, :]).then_inc(summed, 1)
                            else:
                                dve.wait_ge(summed, n)
                                dve.tensor_tensor(acc[:, :], acc[:, :], sq[:, n % 2, :], ALU.add).then_inc(summed, 1)

                    def norm_split(nu, width):
                        dve.wait_ge(summed, SQ0[nu + 1])
                        if nu:
                            dve.wait_ge(sum_all, nu)
                        dve.tensor_copy(acc_hi[:, :], acc[:, :]).then_inc(sum_split, 1)
                        dve.wait_ge(sum_split, 2 * nu + 1)
                        dve.tensor_tensor(acc_lo[:, :], acc[:, :], acc_hi[:, :].bitcast(F32), ALU.subtract)\
                           .then_inc(sum_split, 1)

                    def norm_refine(nu, width):
                        dve.wait_ge(rs_guess, 2 * nu + 1)
                        dve.tensor_scalar(ms[:, :], norm_bank[:, :], 1.0 / width, EPS, ALU.mult, ALU.add)\
                           .then_inc(rs_step, 1)
                        dve.wait_ge(rs_guess, 2 * nu + 2)
                        dve.tensor_tensor(rst[:, :], rs0[:, :], rs0[:, :], ALU.mult).then_inc(rs_step, 1)
                        dve.wait_ge(rs_step, 4 * nu + 2)
                        dve.scalar_tensor_tensor(out=rst[:, :], in0=rst[:, :], scalar=-0.5, in1=ms[:, :],
                                                 op0=ALU.mult, op1=ALU.mult).then_inc(rs_step, 1)
                        dve.wait_ge(rs_step, 4 * nu + 3)
                        dve.scalar_tensor_tensor(out=rstd[:, :], in0=rst[:, :], scalar=1.5, in1=rs0[:, :],
                                                 op0=ALU.add, op1=ALU.mult).then_inc(rs_step, 1)
                        dve.wait_ge(rs_step, 4 * nu + 4)

                    def normalize(n0, tiles, src, gain, his, los):
                        def scaled(i):
                            n = n0 + i
                            if n > 1:
                                dve.wait_ge(hlo, n - 1)
                            dve.scalar_tensor_tensor(out=hf[:, n % 2, :], in0=src(i), scalar=vec[:, gain + i:gain + i + 1],
                                                     in1=rstd[:, :], op0=ALU.mult, op1=ALU.mult).then_inc(hf_set, 1)

                        scaled(0)
                        for i in range(tiles):
                            n = n0 + i
                            if i + 1 < tiles:
                                scaled(i + 1)
                            dve.wait_ge(hhi, n + 1)
                            dve.tensor_tensor(los(i), hf[:, n % 2, :], his(i).bitcast(F32), ALU.subtract)\
                               .then_inc(hlo, 1)

                    def residual(n0, gain):
                        for t in range(KT):
                            n = 2 * (n0 + t)
                            if n > 2:
                                dve.wait_ge(res, n - 2)
                            dve.scalar_tensor_tensor(out=hf[:, t % 2, :], in0=y[:, t, :], scalar=vec[:, gain + t:gain + t + 1],
                                                     in1=rstd[:, :], op0=ALU.mult, op1=ALU.mult).then_inc(res, 1)
                            dve.wait_ge(res, n + 1)
                            dve.tensor_tensor(x[:, t, :], x[:, t, :], hf[:, t % 2, :], ALU.add).then_inc(res, 1)

                    def tile_ready(k):
                        dve.wait_ge(full, k + 1)

                    def low(k, dst, src, hi, after, scale=1.0):
                        dve.wait_ge(after[0], after[1])
                        if scale == 1.0:
                            ins = dve.tensor_tensor(dst, src, hi.bitcast(F32), ALU.subtract)
                        else:
                            ins = dve.scalar_tensor_tensor(out=dst, in0=src, scalar=scale, in1=hi.bitcast(F32),
                                                           op0=ALU.mult, op1=ALU.subtract)
                        ins.then_inc(free[k % 2], 1)

                    def probs_lo(n, src, hi, lo):
                        dve.wait_ge(p_h, n + 1)
                        dve.tensor_tensor(lo, src, hi.bitcast(F32), ALU.subtract).then_inc(p_l, 1)

                    def biggest(n, base, order, banks, to):
                        m = 4 * n
                        banded = order is not CAUSAL
                        last = n - 1 if banded and n > HEADS else n
                        if last > 0:
                            dve.wait_ge(mx_all, last)
                        for i, (j, q0, w, b, col) in enumerate(order):
                            dve.wait_ge(score_full, base + b + 1)
                            if i:
                                dve.wait_ge(mx_step, m + i)
                            src = banks[b][:, col:col + w]
                            if i == 0 or (banded and i == 1):
                                ins = dve.tensor_copy(to[:, q0:q0 + w], src)
                            else:
                                ins = dve.tensor_tensor(to[:, q0:q0 + w], src, to[:, q0:q0 + w], ALU.max)
                            ins.then_inc(mx_step, 1)

                    def subtract(n, pieces, banks, to, biggest_):
                        if n > 0:
                            dve.wait_ge(p_l, n)
                        for i, (j, q0, w, b, col) in enumerate(pieces):
                            s0 = b * SEQ + col if pieces is CAUSAL else 2 * q0
                            ins = dve.tensor_tensor(to[:, s0:s0 + w], banks[b][:, col:col + w],
                                                    biggest_[:, q0:q0 + w], ALU.subtract)
                        ins.then_inc(sub, 1)
                        dve.wait_ge(sub, n + 1)
                        dve.sem_inc(score_free, 1)

                    def soft_out(n):
                        dve.wait_ge(den_inv, 2 * n + 2)
                        rows = slice(HEAD * (n % 2), HEAD * (n % 2 + 1))
                        if n > 1:
                            dve.wait_ge(o_l, n // 2)
                        dve.tensor_tensor(of[rows, :], pv_bank[0:HEAD, :], dn[0:HEAD, :], ALU.mult)\
                           .then_inc(pv_free, 1)

                    def out_lo(n):
                        m = n // 2
                        b, q = m // PAIRS, m % PAIRS
                        dve.wait_ge(o_h, m + 1)
                        dve.tensor_tensor(o_lo[b][:, q, :], of[:, :], o_hi[b][:, q, :].bitcast(F32), ALU.subtract)\
                           .then_inc(o_l, 1)

                    dve.tensor_copy(vec[:, :], vec_all[:, bass.ds(l * VECS, VECS)]).then_inc(vec_set, 1)
                    dve.wait_ge(vec_set, 1)
                    gather(PRE, 0, KT, 0)
                    norm_split(PRE, D)
                    split(0)
                    split(1)
                    norm_refine(PRE, D)
                    normalize(0, KT, lambda i: x[:, i, :], V_PRE, lambda i: h_hi[:, i, :], lambda i: h_lo[:, i, :])
                    for i in range(4):
                        split(C_LATENT + i + 2)
                    tile_ready(3)
                    dve.tensor_tensor(ra[HEAD:P, :], proj[1][0:HEAD, :], KCOS[HEAD:P, :], ALU.mult)\
                       .then_inc(kr_part, 1)
                    dve.tensor_tensor(rb[HEAD:P, :], proj[1][HEAD:P, :], KSIN[HEAD:P, :], ALU.mult)\
                       .then_inc(free[1], 1)
                    dve.wait_ge(kr_part, 1)
                    dve.wait_ge(free[1], 2)
                    dve.tensor_tensor(ra[HEAD:P, :], ra[HEAD:P, :], rb[HEAD:P, :], ALU.add).then_inc(kr_sum, 1)
                    gather(QLAT, 0, 2, SQ0[QLAT])
                    norm_split(QLAT, Q_LORA)
                    gather(KVLAT, 0, 1, SQ0[KVLAT])
                    norm_refine(QLAT, Q_LORA)
                    normalize(8, 2, lambda i: cf[:, i, :], V_Q, lambda i: cqn_hi[:, i, :], lambda i: cqn_lo[:, i, :])
                    norm_split(KVLAT, KV_LORA)
                    norm_refine(KVLAT, KV_LORA)
                    normalize(10, 1, lambda i: cf[:, 2, :], V_KV, lambda i: ckn_hi[:, :], lambda i: ckn_lo[:, :])
                    for s in range(2):
                        dve.wait_ge(kr_hi, s + 1)
                        dve.tensor_tensor(mk_lo[HEAD:P, s, :], ra[HEAD:P, :], mk_hi[HEAD:P, s, :].bitcast(F32),
                                          ALU.subtract).then_inc(kr_lo, 1)

                    def mla_qk(h):
                        k, s = A_MLA + 3 * h, h % 2
                        if h % 2 == 0:
                            split(C_MLA + h // 2 + 2)
                        tile_ready(k)
                        if h:
                            dve.wait_ge(mq_l, h)
                        dve.tensor_tensor(mqf[:, :], proj[k % 2][:, :], QPE, ALU.mult).then_inc(mq_f, 1)
                        dve.wait_ge(mq_f, h + 1)
                        dve.sem_inc(free[k % 2], 1)
                        dve.wait_ge(mq_h, h + 1)
                        dve.tensor_tensor(mq_lo[:, s, :], mqf[:, :], mq_hi[:, s, :].bitcast(F32), ALU.subtract)\
                           .then_inc(mq_l, 1)
                        low(k + 1, mk_lo[0:HEAD, s, :], proj[(k + 1) % 2][0:HEAD, :], mk_hi[0:HEAD, s, :], (mk_h, h + 1))

                    def mla_v(h):
                        k, s = A_MLA + 3 * h + 2, h % 2
                        low(k, mv_lo[:, s, :, 0:HEAD],
                            proj[k % 2][:, 0:NB * HEAD].rearrange("p (j d) -> p j d", j=NB), mv_hi[:, s, :, 0:HEAD],
                            (mv_h, h + 1))

                    def mla_biggest(h):
                        biggest(h, 3 * h, CAUSAL, score, mx)

                    def mla_subtract(h):
                        dve.wait_ge(mx_all, h + 1)
                        subtract(h, CAUSAL, score, s_f, mxr)

                    mla_qk(0)
                    mla_v(0)
                    mla_biggest(0)
                    mla_qk(1)
                    mla_v(1)
                    mla_subtract(0)
                    for h in range(HEADS):
                        if h + 1 < HEADS:
                            mla_biggest(h + 1)
                        probs_lo(h, s_f[:, :], p_hi[:, :], p_lo[:, :])
                        if h + 2 < HEADS:
                            mla_qk(h + 2)
                        if h + 1 < HEADS:
                            mla_subtract(h + 1)
                        soft_out(h)
                        if h + 2 < HEADS:
                            mla_v(h + 2)
                        if h % 2:
                            out_lo(h)

                    def rope(n, k, scale, dst, hi):
                        dve.wait_ge(rp_h, n + 1)
                        if n:
                            dve.wait_ge(rot, n)
                        if scale == 1.0:
                            dve.tensor_tensor(rp_lo[:, :], proj[k % 2][:, :], rp_hi[:, :].bitcast(F32), ALU.subtract)\
                               .then_inc(rp_l, 1)
                        else:
                            dve.scalar_tensor_tensor(out=rp_lo[:, :], in0=proj[k % 2][:, :], scalar=scale,
                                                     in1=rp_hi[:, :].bitcast(F32), op0=ALU.mult, op1=ALU.subtract)\
                               .then_inc(rp_l, 1)
                        if n:
                            dve.wait_ge(rpo_l, n)
                        dve.scalar_tensor_tensor(out=ra[:, :], in0=proj[k % 2][:, :], scalar=scale, in1=COS,
                                                 op0=ALU.mult, op1=ALU.mult).then_inc(free[k % 2], 1)
                        dve.wait_ge(rot, n + 1)
                        if n:
                            dve.wait_ge(rp_sum, n)
                        dve.tensor_tensor(rb[:, :], rot_bank[:, :], SIN, ALU.mult).then_inc(rot_used, 1)
                        dve.wait_ge(rot_used, n + 1)
                        dve.wait_ge(free[k % 2], k // 2 + 1)
                        dve.tensor_tensor(ra[:, :], ra[:, :], rb[:, :], ALU.add).then_inc(rp_sum, 1)
                        dve.wait_ge(rpo_h, n + 1)
                        dve.tensor_tensor(dst, ra[:, :], hi.bitcast(F32), ALU.subtract).then_inc(rpo_l, 1)

                    split(C_SWA + 2)
                    rope(0, A_SWA, 1.0, wk_lo[:, :], wk_hi[:, :])
                    split(C_SWA + 3)
                    low(A_SWA + 1, wv_lo[:, :, :, 0:HEAD],
                        proj[(A_SWA + 1) % 2][:, :].rearrange("p (j v d) -> p j v d", j=NB, v=2),
                        wv_hi[:, :, :, 0:HEAD], (wv_h, 1))
                    for t in range(PAIRS):
                        split(C_SWA + 4 + t)
                        rope(t + 1, A_SWA + 2 + t, 0.125, wq_lo[:, t, :], wq_hi[:, t, :])
                    def band_biggest(n):
                        biggest(HEADS + n, 3 * HEADS + 2 * n, [BANDED[0], BANDED[2], BANDED[1], BANDED[3]], band[n % 2],
                                bmx[n % 2])

                    dve.wait_ge(pv_full, HEADS)
                    band_biggest(0)
                    band_biggest(1)
                    for n in range(HEADS + 1):
                        if n < HEADS:
                            head = n // 2 + 4 * (n % 2)
                            dve.wait_ge(mx_all, HEADS + n + 1)
                            dve.tensor_scalar(bmxr[n % 2][:, :], bmxr[n % 2][:, :],
                                              vec[:, V_SINK + head:V_SINK + head + 1], None, ALU.max).then_inc(mx_sink, 1)
                            dve.wait_ge(mx_sink, n + 1)
                            subtract(HEADS + n, BANDED, band[n % 2], bs_f, bmxr[n % 2])
                        if n:
                            dve.wait_ge(pv_full, HEADS + n)
                            dve.wait_ge(sink_e, n)
                            dve.tensor_tensor(dn[HEAD:P, :], pv_bank[HEAD:P, :], dn[HEAD:P, :], ALU.add)\
                               .then_inc(den, 1)
                        if n + 2 < HEADS:
                            band_biggest(n + 2)
                        if n < HEADS:
                            probs_lo(HEADS + n, bs_f[:, :], bp_hi[:, :], bp_lo[:, :])
                        if n:
                            soft_out(HEADS + n - 1)
                        if n and n % 2 == 0:
                            out_lo(HEADS + n - 1)

                    def stick_in(p, i):
                        c, k, s = C_SB + 3 * p + i, A_SB + 3 * p + i, p % 2
                        split(c + 2)
                        low(k, sb_lo[s][:, i, :], proj[k % 2][:, :], sb_hi[s][:, i, :], (sbh, 3 * p + i + 1),
                            0.125 if i == 0 else 1.0)

                    def stick_min(h):
                        for b, w in enumerate(STICK_COLS):
                            dve.wait_ge(score_full, 5 * HEADS + 5 * (h // 2) + (3 if b == 2 else b + 1 + 3 * (h % 2)))
                            if b == 0:
                                dve.wait_ge(p_l, 2 * HEADS + max(h - 1, 0))
                                if h < 2:
                                    dve.wait_ge(pv_full, 2 * HEADS)
                            src, off = stick[h % 2][b]
                            dve.tensor_scalar(fb[h % 2][:, b * SEQ:b * SEQ + w], src[:, off:off + w], 40.0, None, ALU.min)\
                               .then_inc(z_min, 1)

                    def stick_max(h):
                        dve.wait_ge(z_ln, h + 1)
                        for b, w in enumerate(STICK_COLS):
                            src, off = stick[h % 2][b]
                            to = fb[h % 2][:, b * SEQ:b * SEQ + w]
                            dve.tensor_tensor(to, src[:, off:off + w], to, ALU.max).then_inc(z_max, 1)

                    def stick_lo(h):
                        dve.wait_ge(sp_h, h + 1)
                        dve.tensor_tensor(sp_lo[:, :], fb[h % 2][:, :], sp_hi[:, :].bitcast(F32), ALU.subtract)\
                           .then_inc(sp_l, 1)

                    def stick_out(h):
                        rows = slice(HEAD * (h % 2), HEAD * (h % 2 + 1))
                        dve.wait_ge(sbo_h, h + 1)
                        dve.tensor_tensor(o_lo[2][rows, h // 2, :], pv_bank[rows, :], o_hi[2][rows, h // 2, :].bitcast(F32),
                                          ALU.subtract).then_inc(pv_free, 1)

                    for i in range(3):
                        stick_in(0, i)
                    for p in range(PAIRS):
                        h, more = 2 * p, p + 1 < PAIRS
                        stick_min(h)
                        stick_min(h + 1)
                        stick_max(h)
                        if p:
                            stick_out(h - 1)
                        stick_max(h + 1)
                        if more:
                            stick_in(p + 1, 0)
                        stick_lo(h)
                        if more:
                            stick_in(p + 1, 1)
                        stick_lo(h + 1)
                        probs_lo(2 * HEADS + h, fb[0][:, :], p_hi[:, :], p_lo[:, :])
                        if more:
                            stick_in(p + 1, 2)
                        stick_out(h)
                        probs_lo(2 * HEADS + h + 1, fb[1][:, :], p_hi[:, :], p_lo[:, :])
                    stick_out(HEADS - 1)

                    for kind, b, t, c, i, n in merge_plan():
                        if i == 0:
                            split(c + 2)
                        if kind == "o":
                            continue
                        k = A_GATE + n
                        dve.wait_ge(merge_full, n + 1)
                        dve.wait_ge(free[k % 2], k // 2 + 1)
                        m = 4 * (t // 2) + 2 * (b - 1) + t % 2
                        if b == 0:
                            if t > 1:
                                dve.wait_ge(mix_l, t - 1)
                            dve.tensor_tensor(mix[:, t % 2, :], merge_bank[n % 2][:, :], gate[:, n % 2, :], ALU.mult)\
                               .then_inc(merge_free[n % 2], 1)
                        else:
                            if m:
                                dve.wait_ge(mix_add, m)
                            dve.tensor_tensor(prod[:, :], merge_bank[n % 2][:, :], gate[:, n % 2, :], ALU.mult)\
                               .then_inc(merge_free[n % 2], 1)
                            dve.wait_ge(merge_free[n % 2], n // 2 + 1)
                            dve.tensor_tensor(mix[:, t % 2, :], mix[:, t % 2, :], prod[:, :], ALU.add)\
                               .then_inc(mix_add, 1)
                        if b == 2 and t % 2:
                            for t2 in (t - 1, t):
                                dve.wait_ge(mix_h, t2 + 1)
                                dve.tensor_tensor(mix_lo[:, t2, :], mix[:, t2 % 2, :], mix_hi[:, t2, :].bitcast(F32),
                                                  ALU.subtract).then_inc(mix_l, 1)

                    for t in range(KT):
                        split(C_OUT + t + 2)
                        n = SQ0[POST] + t
                        dve.wait_ge(squared, n + 1)
                        if t == 0:
                            dve.tensor_copy(acc[:, :], sq[:, n % 2, :]).then_inc(summed, 1)
                        else:
                            dve.wait_ge(summed, n)
                            dve.tensor_tensor(acc[:, :], acc[:, :], sq[:, n % 2, :], ALU.add).then_inc(summed, 1)
                    norm_split(POST, D)
                    norm_refine(POST, D)
                    residual(0, V_POST)
                    gather(MPRE, 0, KT, SQ0[MPRE])
                    norm_split(MPRE, D)
                    norm_refine(MPRE, D)
                    normalize(H0[MPRE], KT, lambda i: x[:, i, :], V_MPRE, lambda i: h_hi[:, i, :],
                              lambda i: h_lo[:, i, :])

                    k = 0
                    for what, g in MLP:
                        for t in range(KT):
                            kk = A_MLP + k
                            split(C_MLP + k + 2)
                            if what == "up":
                                n = KT * g + t
                                dve.wait_ge(free[kk % 2], kk // 2 + 1)
                                if n > 1:
                                    dve.wait_ge(u_l, n - 1)
                                dve.tensor_tensor(usq[:, n % 2, :], relu[:, n % 2, :], relu[:, n % 2, :], ALU.mult)\
                                   .then_inc(u_s, 1)
                                dve.wait_ge(u_h, n + 1)
                                dve.wait_ge(u_s, n + 1)
                                dve.tensor_tensor(u_lo[g % 2][:, t, :], usq[:, n % 2, :],
                                                  u_hi[g % 2][:, t, :].bitcast(F32), ALU.subtract).then_inc(u_l, 1)
                            else:
                                tile_ready(kk)
                                if g == 0:
                                    ins = dve.tensor_copy(y[:, t, :], proj[kk % 2][:, :])
                                else:
                                    kp = kk - (2 * KT if g < GROUPS - 1 else KT)
                                    dve.wait_ge(free[kp % 2], kp // 2 + 1)
                                    ins = dve.tensor_tensor(y[:, t, :], proj[kk % 2][:, :], y[:, t, :], ALU.add)
                                ins.then_inc(free[kk % 2], 1)
                                if g == GROUPS - 1:
                                    n = SQ0[MPOST] + t
                                    dve.wait_ge(squared, n + 1)
                                    if t == 0:
                                        dve.tensor_copy(acc[:, :], sq[:, n % 2, :]).then_inc(summed, 1)
                                    else:
                                        dve.wait_ge(summed, n)
                                        dve.tensor_tensor(acc[:, :], acc[:, :], sq[:, n % 2, :], ALU.add)\
                                           .then_inc(summed, 1)
                            k += 1
                    norm_split(MPOST, D)
                    norm_refine(MPOST, D)
                    residual(8, V_MPOST)

                @block.gpsimd
                def _(pool):
                    pool.wait_ge(full, 1)
                    pool.memset(mv_hi[:, :, :, HEAD:P].bitcast(F32), 1.0).then_inc(ones_set, 1)
                    pool.memset(mv_lo[:, :, :, HEAD:P].bitcast(F32), 0.0).then_inc(ones_set, 1)
                    for n in range(HEADS):
                        pool.wait_ge(mx_step, 4 * n + 4)
                        if n:
                            pool.wait_ge(score_free, n)
                        pool.partition_all_reduce(mxr[:, :], mx[:, :], P, bass.bass_isa.ReduceOp.max)\
                            .then_inc(mx_all, 1)
                    pool.wait_ge(full, A_SWA + 1)
                    pool.memset(wv_hi[:, :, :, HEAD:P].bitcast(F32), 1.0).then_inc(ones_set, 1)
                    pool.memset(wv_lo[:, :, :, HEAD:P].bitcast(F32), 0.0).then_inc(ones_set, 1)
                    for n in range(HEADS, 2 * HEADS):
                        pool.wait_ge(mx_step, 4 * n + 4)
                        if n > HEADS + 1:
                            pool.wait_ge(score_free, n - 1)
                            pool.wait_ge(sink_e, n - HEADS - 1)
                        pool.partition_all_reduce(bmxr[n % 2][:, :], bmx[n % 2][:, :], P, bass.bass_isa.ReduceOp.max)\
                            .then_inc(mx_all, 1)
                    for h in range(HEADS):
                        pool.wait_ge(z_max, 3 * h + 3)
                        for off in (0, 512, 896, 1024):
                            to = fb[h % 2][:, off:off + P]
                            pool.tensor_tensor(to, to, tri01[:, :], ALU.mult).then_inc(z_mask, 1)

            numbers = [s.num for s in cleared]
            assert numbers == list(range(numbers[0], numbers[0] + len(numbers)))
            nc.all_engine_barrier(sems_to_clear=range(numbers[0], numbers[-1] + 1))

        with nc.Block() as block:

            @block.sync
            def _(sp):
                sp.dma_start(out, x[:, :, :]).then_inc(stored, 16)
                sp.wait_ge(stored, 16)


def constants():
    p, c = np.arange(P)[:, None], np.arange(P)[None, :]
    swap = np.where(p % HEAD < HEAD // 2, p + HEAD // 2, p - HEAD // 2)
    mats = [p == c, swap == c, -(p >= c).astype(np.float32), -np.ones((P, P)), np.ones((P, P)),
            -BIG * (c > p), -BIG * (c >= p), -BIG * (c <= p), p < c]
    const = np.concatenate([np.asarray(m, np.float32) for m in mats], axis=1)

    def inv(d):
        return (1.0 / (np.float32(THETA) ** (np.arange(0, d, 2, dtype=np.float32) / np.float32(d)))).astype(np.float32)

    row = np.arange(P)
    full, part = inv(HEAD)[row % (HEAD // 2)], inv(ROPE_DIM)[row % (ROPE_DIM // 2)]
    sign_full = np.where(row % HEAD < HEAD // 2, -1.0, 1.0)
    sign_part = np.where(row % ROPE_DIM < ROPE_DIM // 2, -1.0, 1.0)
    q, one, zero = 0.25, np.ones(P), np.zeros(P)
    upper = row >= 3 * ROPE_DIM
    trig = [(full, q * one, one), (full, zero, sign_full),
            (part, np.where(upper, 0, q), np.where(upper, sign_part, 1.0)),
            (part, q * one, one), (part, zero, sign_part)]
    cols = [v for f, ph, s in trig for v in (f, ph, ph * 2 * np.pi, s)]
    return const, np.stack(cols, axis=1).astype(np.float32)


def chunk(w, cols):
    w = w[:, cols]
    return w.reshape(-1, P, P).transpose(1, 0, 2).reshape(P, -1)


def weight_stream(w_in, w_uq, w_ukv, w_o, w_out, w_up, w_down):
    r = np.arange
    kr = 384 + r(ROPE_DIM)
    krs = np.roll(kr, ROPE_DIM // 2)
    cs = [chunk(w_in, r(128 * i, 128 * i + 128)) for i in range(3)]
    cs.append(chunk(w_in, np.concatenate([kr, kr, krs, krs])))
    for p in range(PAIRS):
        part = []
        for h in (2 * p, 2 * p + 1):
            pe = 96 * h + 64 + r(32)
            q = np.concatenate([96 * h + r(64), pe, np.roll(pe, 16)])
            part += [chunk(w_uq, q), chunk(w_ukv, 128 * h + r(128))]
        part.append(np.zeros((P, CH - 6 * P), np.float32))
        cs.append(np.concatenate(part, axis=1))
    cs.append(chunk(w_in, 928 + r(128)))
    cs.append(chunk(w_in, 1056 + r(128)))
    both = [np.concatenate([64 * t + r(64), 64 * (t + 4) + r(64)]) for t in range(PAIRS)]
    cs += [chunk(w_in, 416 + both[t]) for t in range(PAIRS)]
    for p in range(PAIRS):
        cs += [chunk(w_in, o + 128 * p + r(128)) for o in (1184, 1696, 2208)]
    w_o = [w_o[0], w_o[1][np.concatenate(both)], w_o[2]]
    for u in range(KT // 2):
        for b in range(3):
            g = [chunk(w_in, 2720 + D * b + P * t + r(P)) for t in (2 * u, 2 * u + 1)]
            o = [chunk(w_o[b], P * t + r(P)) for t in (2 * u, 2 * u + 1)]
            cs += [g[0], np.concatenate(o, axis=1), g[1]]
    cs += [chunk(w_out, P * t + r(P)) for t in range(KT)]
    up = [[chunk(w_up, D * g + P * t + r(P)) for t in range(KT)] for g in range(GROUPS)]
    down = [[chunk(w_down[D * g:D * (g + 1)], P * t + r(P)) for t in range(KT)] for g in range(GROUPS)]
    cs += up[0]
    for g in range(GROUPS):
        if g + 1 < GROUPS:
            cs += up[g + 1]
        cs += down[g]
    return np.stack(cs)


def kernel(**inputs):
    import numpy as _np
    import concourse.bacc as _bacc
    from concourse import mybir as _mybir
    from concourse.bass_utils import run_bass_kernel_spmd as _run

    a = {k: _np.asarray(v) for k, v in inputs.items()}
    w = _np.stack([weight_stream(a["w_in"][l], a["w_uq"][l], a["w_ukv"][l],
                                 [a["w_o_mla"][l], a["w_o_swa"][l], a["w_o_sb"][l]],
                                 a["w_out"][l], a["w_up"][l], a["w_down"][l]) for l in range(DEPTH)])
    vecs = []
    for l in range(DEPTH):
        for n in ("g_mix_pre", "b_gate", "g_q_lat", "g_kv_lat", "g_mix_post", "g_mlp_pre", "g_mlp_post"):
            vecs.append(a[n][l].reshape(-1, P).T)
        vecs.append(_np.broadcast_to(a["swa_sinks"][l][None, :], (P, HEADS)))
    const, trig = constants()
    arrays = {
        "x": _np.ascontiguousarray(a["x"][0].T.reshape(KT, P, SEQ).transpose(1, 0, 2)),
        "pos": _np.ascontiguousarray(a["positions"]),
        "w": w, "vec": _np.ascontiguousarray(_np.concatenate(vecs, axis=1)),
        "const": const, "trig": trig,
    }
    nc = _bacc.Bacc("TRN2", target_bir_lowering=False, num_devices=1)
    args = [nc.dram_tensor(f"in_{n}", v.shape, _mybir.dt.from_np(v.dtype), kind="ExternalInput").ap()
            for n, v in arrays.items()]
    out = nc.dram_tensor("out_y", (P, KT, SEQ), F32, kind="ExternalOutput").ap()
    trunk(nc, *args, out)
    r = _run(nc, [{f"in_{n}": v for n, v in arrays.items()}], core_ids=[0])
    got = r.results[0]["out_y"]
    return got.transpose(1, 0, 2).reshape(D, SEQ).T.reshape(1, SEQ, D)
```

```python
from contextlib import ExitStack

import concourse.bass as bass
import numpy as np
from concourse import mybir

ALU = mybir.AluOpType
ACT = mybir.ActivationFunctionType
F32 = mybir.dt.float32
F32R = mybir.dt.float32r
I32 = mybir.dt.int32

P = 128
DEPTH, D, SEQ = 2, 1024, 512
HEADS, HEAD = 8, 64
ROPE_DIM, Q_LORA, KV_LORA = 32, 256, 128
D_FF = 4096
WINDOW = 128
EPS = 1e-6
THETA = 10000.0
KT = D // P
NB = SEQ // P
PAIRS = HEADS // 2
CH = KT * P
GROUPS = D_FF // D

RING = 3


def order():
    def mla(h, kinds):
        return [((kind, h), ("mla", h)) for kind in kinds]

    def own(*name):
        return [(name, name)]

    def turned(*name):
        return [(name, None)]

    def o(b, t):
        return [(("o", b, t), ("o", b, t // 2))]

    seq = [e for i in range(4) for e in own("latent", i)]
    for h in range(2):
        seq += own("gate", 0, h) + mla(h, ("mla_q", "mla_k", "mla_v"))
    for h in range(2, HEADS):
        seq += mla(h, ("mla_q", "mla_k", "mla_v")) + own("gate", 0, h)
    seq += own("swa_k") + own("swa_vt") + own("swa_q", 0) + turned("swa_v")
    seq += [e for t in range(1, PAIRS) for e in own("swa_q", t)]
    seq += own("stick", 0, 0) + own("stick", 0, 1)
    for n in range(HEADS):
        seq += o(0, n)
    seq += own("stick_vt", 0) + turned("stick", 0, 2)
    for p in range(PAIRS):
        more = p + 1 < PAIRS
        seq += own("stick", p + 1, 0) + own("stick", p + 1, 1) if more else own("gate", 2, 0) + own("gate", 2, 1)
        seq += (own("stick_vt", p + 1) if more else own("gate", 2, 2)) + own("gate", 1, 2 * p)
        seq += (turned("stick", p + 1, 2) if more else own("gate", 2, 3)) + own("gate", 1, 2 * p + 1)
        seq += o(1, 2 * p) + o(1, 2 * p + 1)
    for t in range(0, KT, 2):
        seq += (own("gate", 2, t) + own("gate", 2, t + 1) if t > 3 else []) + o(2, t) + o(2, t + 1)
    seq += [e for t in range(KT) for e in own("out", t)]
    seq += [e for t in range(KT) for e in own("up", 0, t)]
    for g in range(GROUPS):
        if g + 1 < GROUPS:
            seq += [e for t in range(KT) for e in own("up", g + 1, t)]
        seq += [e for t in range(KT) for e in own("down", g, t)]
    return seq


ORDER = order()
T = {tile: k for k, (tile, _) in enumerate(ORDER)}
TILES = len(T)
C, LAST = {}, []
for _, _chunk in ORDER:
    if _chunk and _chunk not in C:
        C[_chunk] = len(C)
CHUNKS = len(C)
LAST = [max(T[tile] for tile, chunk in ORDER if chunk and C[chunk] == c) for c in range(CHUNKS)]
WIDTH = [3 * P if name[0] == "mla" else CH for name in C]
BY_GPSIMD = [name[:2] == ("gate", 0) and name != ("gate", 0, 0) and name != ("gate", 0, 1) for name in C]
LOWS = [sum(BY_GPSIMD[i] == BY_GPSIMD[c] for i in range(c + 1)) for c in range(CHUNKS)]
V_PRE, V_GATE, V_Q, V_KV, V_POST, V_MPRE, V_MPOST, V_SINK = 0, 8, 32, 34, 35, 43, 51, 59
VECS = V_SINK + HEADS
IDENT, SWAP, NEG_TRI, NEG_ONE, ONE, MASK_CAUSAL, MASK_STRICT, MASK_PREV, TRI01 = range(9)
N_CONST = 9 * P
TRIG = 4 * 5
TABLES = (1, 0, 4, 3, 2)
PI_BELOW = 3.1415925
BIG = 1e30
TWO_PI = float(2 * np.pi)


def pi_parts():
    left, parts = 2 * np.pi, []
    for _ in range(3):
        e = 2.0 ** (7 - np.floor(np.log2(left)))
        part = np.floor(left * e) / e
        parts.append(float(part))
        left -= part
    return parts + [float(left)]


CAUSAL = [(0, 0, 512, 0, 0), (1, 128, 384, 1, 0), (3, 384, 128, 1, 384), (2, 256, 256, 2, 0)]
BANDED = [(0, 0, 256, 0, 0), (1, 128, 256, 0, 256), (2, 256, 256, 1, 0), (3, 384, 128, 1, 256)]
CAUSAL_COLS, BANDED_COLS = 1280, 896

NORMS = [8, 2, 1, 8, 8, 8]
SQ0 = [sum(NORMS[:i]) for i in range(7)]
PRE, QLAT, KVLAT, POST, MPRE, MPOST = range(6)
assert WINDOW == P, "a block sees itself and the one before it"


def trunk(nc, A_x, A_pos, A_w, A_vec, A_const, A_trig, out):
    with ExitStack() as ctx:
        at = [nc.sbuf_base + (-nc.sbuf_base) % 32]

        def place(name, shape, dt, offset=None):
            size = int(np.prod(shape[1:])) * 4
            if offset is None:
                offset = at[0]
                at[0] += size + (-size) % 32
            return nc.alloc_sbuf_tensor_at(name, shape, dt, offset=offset)

        def sem(name):
            return ctx.enter_context(nc.semaphore(name))

        h_hi, h_lo = (place(n, [P, KT, SEQ], F32R) for n in ("h_hi", "h_lo"))
        x = place("x", [P, KT, SEQ], F32)
        raw = place("raw", [P, RING, CH], F32)
        w_hi, w_lo = (place(n, [P, RING, CH], F32R) for n in ("w_hi", "w_lo"))
        tab = place("tab", [P, 5, SEQ], F32)
        cst = place("cst", [P, 8, P], F32R)
        tri01 = place("tri01", [P, P], F32)
        vec_all = place("vec_all", [P, DEPTH * VECS], F32)
        vec = place("vec", [P, VECS], F32)
        trig = place("trig", [P, TRIG], F32)
        r1 = at[0]
        at[0] += 49152
        o_hi, o_lo = [], []
        for b in range(2):
            o_hi.append(place(f"o_hi{b}", [P, PAIRS, SEQ], F32R, r1 + 16384 * b))
            o_lo.append(place(f"o_lo{b}", [P, PAIRS, SEQ], F32R, r1 + 16384 * b + 8192))
        mix = place("mix", [P, KT, SEQ], F32, r1 + 32768)
        u_hi = [place("u_hi0", [P, KT, SEQ], F32R, r1)]
        u_lo = [place("u_lo0", [P, KT, SEQ], F32R, r1 + 16384)]
        y = place("y", [P, KT, SEQ], F32, r1 + 32768)
        r2 = at[0]
        at[0] += 36864
        cqn_hi = place("cqn_hi", [P, 2, SEQ], F32R, r2)
        cqn_lo = place("cqn_lo", [P, 2, SEQ], F32R, r2 + 4096)
        ckn_hi = place("ckn_hi", [P, SEQ], F32R, r2 + 8192)
        ckn_lo = place("ckn_lo", [P, SEQ], F32R, r2 + 10240)
        mq_hi = place("mq_hi", [P, 2, SEQ], F32R, r2 + 12288)
        mq_lo = place("mq_lo", [P, 2, SEQ], F32R, r2 + 16384)
        mk_hi = place("mk_hi", [P, 2, SEQ], F32R, r2 + 20480)
        mk_lo = place("mk_lo", [P, 2, SEQ], F32R, r2 + 24576)
        mv_hi = place("mv_hi", [P, 2, NB, P], F32R, r2 + 28672)
        mv_lo = place("mv_lo", [P, 2, NB, P], F32R, r2 + 32768)
        wq_hi = place("wq_hi", [P, PAIRS, SEQ], F32R, r2)
        wq_lo = place("wq_lo", [P, PAIRS, SEQ], F32R, r2 + 8192)
        wk_hi = place("wk_hi", [P, SEQ], F32R, r2 + 16384)
        wk_lo = place("wk_lo", [P, SEQ], F32R, r2 + 18432)
        wv_hi = place("wv_hi", [P, NB, 2, P], F32R, r2 + 20480)
        wv_lo = place("wv_lo", [P, NB, 2, P], F32R, r2 + 24576)
        sb_hi = [place(f"sb_hi{s}", [P, 3, SEQ], F32R, r2 + 12288 * s) for s in range(2)]
        sb_lo = [place(f"sb_lo{s}", [P, 3, SEQ], F32R, r2 + 12288 * s + 6144) for s in range(2)]
        sb0_hi = place("sb0_hi", [P, 2, SEQ], F32R, r2 + 28672)
        sb0_lo = place("sb0_lo", [P, 2, SEQ], F32R, r2 + 28672 + 4096)
        gate2 = place("gate2", [P, 4, SEQ], F32, r2)
        vt = [place("vt0", [P, SEQ], F32, r2 + 16384), place("vt1", [P, SEQ], F32, r2 + 34816)]
        sp_hi = place("sp_hi", [P, CAUSAL_COLS], F32R, r2 + 24576)
        sp_lo = place("sp_lo", [P, CAUSAL_COLS], F32R, r2 + 24576 + 5120)
        mix_hi = place("mix_hi", [P, KT, SEQ], F32R, r2)
        mix_lo = place("mix_lo", [P, KT, SEQ], F32R, r2 + 16384)
        u_hi.append(place("u_hi1", [P, KT, SEQ], F32R, r2))
        u_lo.append(place("u_lo1", [P, KT, SEQ], F32R, r2 + 16384))
        cst_f = place("cst_f", [P, N_CONST], F32, r2)
        pos_i = place("pos_i", [P, SEQ], I32, r2 + 8192)
        r3 = at[0]
        at[0] += 24576
        s_f = place("s_f", [P, CAUSAL_COLS], F32, r3)
        p_hi = place("p_hi", [P, CAUSAL_COLS], F32R, r3 + 5120)
        p_lo = place("p_lo", [P, CAUSAL_COLS], F32R, r3 + 10240)
        fb = [place("fb0", [P, CAUSAL_COLS], F32, r3), place("fb1", [P, CAUSAL_COLS], F32, r3 + 15360)]
        mx = place("mx", [P, SEQ], F32, r3 + 15360)
        mxr = place("mxr", [P, SEQ], F32, r3 + 17408)
        bs_f = place("bs_f", [P, BANDED_COLS], F32, r3)
        bp_hi = place("bp_hi", [P, BANDED_COLS], F32R, r3 + 3584)
        bp_lo = place("bp_lo", [P, BANDED_COLS], F32R, r3 + 7168)
        bmx = [place(f"bmx{s}", [P, SEQ], F32, r3 + 10752 + 2048 * s) for s in range(2)]
        bmxr = [place(f"bmxr{s}", [P, SEQ], F32, r3 + 14848 + 2048 * s) for s in range(2)]
        of = place("of", [P, SEQ], F32, r3 + 20480)
        dn = place("dn", [P, SEQ], F32, r3 + 22528)
        sq = place("sq", [P, 2, SEQ], F32, r3)
        acc = place("acc", [P, SEQ], F32, r3 + 4096)
        acc_hi = place("acc_hi", [P, SEQ], F32R, r3 + 6144)
        acc_lo = place("acc_lo", [P, SEQ], F32R, r3 + 8192)
        ms = place("ms", [P, SEQ], F32, r3 + 10240)
        rs0 = place("rs0", [P, SEQ], F32, r3 + 12288)
        rst = place("rst", [P, SEQ], F32, r3 + 14336)
        rstd = place("rstd", [P, SEQ], F32, r3 + 16384)
        hf = place("hf", [P, 3, SEQ], F32, r3 + 18432)
        rsq = place("rsq", [P, SEQ], F32, r3 + 22528)
        gate = place("gate", [P, 2, SEQ], F32, r3 + 20480)
        relu = place("relu", [P, 2, SEQ], F32, r2 + 32768)
        usq = place("usq", [P, 2, SEQ], F32, r3 + 18432)
        cf = place("cf", [P, 3, SEQ], F32, r1 + 16384)
        ra = place("ra", [P, SEQ], F32, r1 + 16384 + 6144)
        rb = place("rb", [P, SEQ], F32, r1 + 16384 + 8192)
        rp_hi = place("rp_hi", [P, SEQ], F32R, r1 + 16384 + 10240)
        rp_lo = place("rp_lo", [P, SEQ], F32R, r1 + 16384 + 12288)
        tables = [place(f"tt{i}", [P, SEQ], F32, r3 + 2048 * i) for i in range(3)]
        COS, SIN, QPE, KCOS, KSIN = (tab[:, i, :] for i in range(5))
        mqf = place("mqf", [P, SEQ], F32, r1 + 16384 + 14336)

        bank = [ctx.enter_context(nc.psum_tensor(f"bank{i}", [P, SEQ], F32)) for i in range(8)]
        proj, score = bank[0:2], bank[2:5]
        pv_bank, rot_bank, norm_bank = bank[5], bank[6], bank[7]
        band = [[bank[2], bank[3]], [bank[4], bank[6]]]
        stick = [[(bank[2], 0), (bank[3], 0), (bank[4], 0)], [(bank[6], 0), (bank[7], 0), (bank[4], 256)]]
        STICK_COLS = (512, 512, 256)

        small_loaded, angles_loaded, angle_set = sem("small_loaded"), sem("angles_loaded"), sem("angle_set")
        stored = sem("stored")
        setup_act, setup_dve = sem("setup_act"), sem("setup_dve")
        cleared = []

        def signal(name):
            cleared.append(sem(name))
            return cleared[-1]

        loaded = [signal(f"loaded{s}") for s in range(RING)]
        whi = signal("w_hi_ready")
        wlo = signal("w_lo_ready")
        wlo_pool = signal("w_lo_by_gpsimd")
        vec_set = signal("vec_set")
        ones_set = signal("ones_set")
        full = signal("tile_full")
        free = [signal(f"tile_free{b}") for b in range(2)]
        squared = signal("squared")
        summed = signal("summed")
        sum_split = signal("sum_split")
        sum_all = signal("sum_all")
        rs_guess = signal("rs_guess")
        rs_step = signal("rs_step")
        hf_set = signal("hf_set")
        hhi = signal("h_hi_ready")
        hlo = signal("h_lo_ready")
        scaled_y = signal("scaled_y")
        res = signal("residual")
        res_even = signal("residual_even")
        xg_hi = signal("xg_hi_ready")
        xg_lo = signal("xg_lo_ready")
        rsq_set = signal("rsq_set")
        y_set = signal("y_set")
        kr_part = signal("kr_part")
        kr_sum = signal("kr_sum")
        kr_hi = signal("kr_hi")
        kr_lo = signal("kr_lo")
        mq_f = signal("mla_q_f")
        mq_h = signal("mla_q_hi")
        mq_l = signal("mla_q_lo")
        mk_h = signal("mla_k_hi")
        mv_h = signal("mla_v_hi")
        rp_h = signal("rope_in_hi")
        rp_l = signal("rope_in_lo")
        rot = signal("rotated")
        rot_used = signal("rot_used")
        rp_sum = signal("rope_sum")
        rpo_h = signal("rope_out_hi")
        rpo_l = signal("rope_out_lo")
        wv_h = signal("swa_v_hi")
        sbh = signal("sb_in_hi")
        score_full = signal("score_full")
        shared_half = signal("shared_half")
        score_free = signal("score_free")
        mx_step = signal("max_step")
        mx_all = signal("max_all")
        mx_sink = signal("max_sink")
        sub = signal("subtracted")
        p_exp = signal("p_exp")
        p_h = signal("p_hi_ready")
        p_l = signal("p_lo_ready")
        pv_full = signal("pv_full")
        pv_free = signal("pv_free")
        sink_e = signal("sink_exp")
        den = signal("denominator")
        den_inv = signal("den_inv")
        o_h = signal("o_hi_ready")
        o_l = signal("o_lo_ready")
        z_min = signal("z_min")
        z_exp = signal("z_exp")
        z_ln = signal("z_ln")
        z_max = signal("z_max")
        z_mask = signal("z_mask")
        sp_h = signal("sp_hi_ready")
        sp_l = signal("sp_lo_ready")
        tail_full = signal("tail_full")
        a_exp = signal("a_exp")
        sbo_h = signal("sb_o_hi")
        mix_add = signal("mix_add")
        mix_gate = signal("mix_gate")
        vt_set = signal("vt_set")
        gate_in = signal("gate_in")
        gate2_in = signal("gate2_in")
        gate_set = signal("gate_set")
        gate_c = signal("gate_c")
        mix_h = signal("mix_hi_ready")
        mix_l = signal("mix_lo_ready")
        u_h = signal("u_hi_ready")
        u_s = signal("u_squared")
        u_l = signal("u_lo_ready")

        def low_ready(c):
            return wlo_pool if BY_GPSIMD[c] else wlo

        def vt_at(p):
            return cf[:, 0, :] if p is None else vt[min(p, 1)][:, :]

        def gated_at(b, t):
            return gate2[:, t, :] if b == 2 and t < 4 else gate[:, t % 2, :]

        def stick_in_hi(p, i):
            return sb0_hi[:, i, :] if p == 0 and i < 2 else sb_hi[p % 2][:, i, :]

        def stick_in_lo(p, i):
            return sb0_lo[:, i, :] if p == 0 and i < 2 else sb_lo[p % 2][:, i, :]

        with nc.Block() as block:

            @block.sync
            def _(sp):
                sp.dma_start(pos_i[:, :], A_pos.broadcast_to([P, SEQ])).then_inc(angles_loaded, 16)
                sp.dma_start(trig[:, :], A_trig).then_inc(angles_loaded, 16)
                sp.dma_start(cst_f[:, :], A_const).then_inc(small_loaded, 16)
                sp.dma_start(vec_all[:, :], A_vec).then_inc(small_loaded, 16)
                sp.dma_start(x[:, :, :], A_x).then_inc(small_loaded, 16)

            @block.scalar
            def _(act):
                for n, i in enumerate(TABLES):
                    act.wait_ge(angle_set, n + 1)
                    act.activation(tab[:, i, :], tab[:, i, :], ACT.Sin).then_inc(setup_act, 1)

            @block.vector
            def _(dve):
                steps = [0]

                def step(ins):
                    steps[0] += 1
                    ins.then_inc(setup_dve, 1)
                    dve.wait_ge(setup_dve, steps[0])

                dve.wait_ge(angles_loaded, 2 * 16)
                parts = pi_parts()
                pos_f, ang, turns = tables[0][:, :], tables[1][:, :], tables[2][:, :]
                step(dve.tensor_copy(pos_f, pos_i[:, :]))
                for i in TABLES:
                    def col(j):
                        return trig[:, 4 * i + j:4 * i + j + 1]

                    to = tab[:, i, :]
                    if i in (1, 4):
                        step(dve.tensor_scalar(ang, pos_f, col(0), None, ALU.mult))
                        step(dve.tensor_scalar(turns, ang, 1.0 / TWO_PI, 12582912.0, ALU.mult, ALU.add))
                        step(dve.tensor_scalar(turns, turns, -12582912.0, None, ALU.add))
                        for part in parts:
                            step(dve.scalar_tensor_tensor(out=ang, in0=turns, scalar=-part, in1=ang,
                                                          op0=ALU.mult, op1=ALU.add))
                        step(dve.tensor_scalar(to, ang, PI_BELOW, -PI_BELOW, ALU.min, ALU.max))
                    else:
                        step(dve.tensor_scalar(turns, ang, col(1), PI_BELOW, ALU.add, ALU.is_gt))
                        step(dve.scalar_tensor_tensor(out=turns, in0=turns, scalar=-TWO_PI, in1=ang,
                                                      op0=ALU.mult, op1=ALU.add))
                        step(dve.tensor_scalar(turns, turns, col(1), PI_BELOW, ALU.add, ALU.min))
                        step(dve.tensor_scalar(to, turns, -PI_BELOW, None, ALU.max))
                    dve.sem_inc(angle_set, 1)
                dve.wait_ge(small_loaded, 3 * 16)
                step(dve.tensor_copy(tri01[:, :], cst_f[:, TRI01 * P:(TRI01 + 1) * P]))
                step(dve.tensor_copy(cst[:, :, :], cst_f[:, 0:8 * P].rearrange("p (a c) -> p a c", a=8)))
                dve.wait_ge(setup_act, 5)
                for i in (1, 2, 4):
                    step(dve.tensor_scalar(tab[:, i, :], tab[:, i, :], trig[:, 4 * i + 3:4 * i + 4], None, ALU.mult))
                step(dve.memset(tab[0:HEAD, 2, :], 1.0))

        with nc.Fori(0, DEPTH) as l:
            with nc.Block() as block:
                @block.sync
                def _(sp):
                    for c in range(CHUNKS):
                        if c >= RING:
                            sp.wait_ge(low_ready(c - RING), LOWS[c - RING])
                        sp.dma_start(raw[:, c % RING, 0:WIDTH[c]], A_w[l, c][:, 0:WIDTH[c]]).then_inc(loaded[c % RING], 16)

                @block.tensor
                def _(pe):

                    def three(o, pairs, start=True, last=True, mm=None):
                        n = len(pairs)
                        for i, ((a, al), (b, bl)) in enumerate(pairs):
                            for j, (s, m) in enumerate(((a, b), (a, bl), (al, b))):
                                mm = pe.matmul(o, s, m, start=start and i == 0 and j == 0,
                                               stop=last and i == n - 1 and j == 2, skip_group_check=True)
                        return mm

                    def add(o, stationary, moving):
                        return pe.matmul(o, stationary, moving, start=False, stop=True, skip_group_check=True)

                    def norm_sum(nu):
                        pe.wait_ge(sum_split, 2 * nu + 2)
                        if nu:
                            pe.wait_ge(rs_step, 4 * (nu - 1) + 1)
                        pe.matmul(norm_bank[:, :], cst[:, ONE, :], acc_hi[:, :], start=True, stop=False)
                        pe.matmul(norm_bank[:, :], cst[:, ONE, :], acc_lo[:, :], start=False, stop=True)\
                          .then_inc(sum_all, 1)

                    def take_bank(k):
                        if k > 1:
                            pe.wait_ge(free[k % 2], k // 2)

                    def weight(c, i):
                        return (w_hi[:, c % RING, i * P:(i + 1) * P], w_lo[:, c % RING, i * P:(i + 1) * P])

                    def tile(name, hi, lo, ready=None):
                        c, k = C[name], T[name]
                        pe.wait_ge(low_ready(c), LOWS[c])
                        take_bank(k)
                        for t in range(KT):
                            if ready:
                                pe.wait_ge(ready[0], ready[1] + t + 1)
                            mm = three(proj[k % 2][:, :], [(weight(c, t), (hi[:, t, :], lo[:, t, :]))],
                                       start=t == 0, last=t == KT - 1)
                        mm.then_inc(full, 1)

                    def two_tiles(a, b, hi, lo, ready):
                        pe.wait_ge(low_ready(C[b]), LOWS[C[b]])
                        take_bank(T[a])
                        take_bank(T[b])
                        for t in range(KT):
                            pe.wait_ge(ready, t + 1)
                            for name in (a, b):
                                mm = three(proj[T[name] % 2][:, :], [(weight(C[name], t), (hi[:, t, :], lo[:, t, :]))],
                                           start=t == 0, last=t == KT - 1)
                                if t == KT - 1:
                                    mm.then_inc(full, 1)

                    def turn(name, n, src):
                        k = T[name]
                        pe.wait_ge(vt_set, n)
                        take_bank(k)
                        for j in range(NB):
                            tok = slice(j * P, (j + 1) * P)
                            mm = pe.matmul(proj[k % 2][:, tok], src[:, tok], cst[:, IDENT, :].bitcast(F32), start=j == 0,
                                           stop=True, skip_group_check=True)
                        mm.then_inc(full, 1)

                    def out_tile(b, t):
                        c, k = C["o", b, t // 2], T["o", b, t]
                        pe.wait_ge(low_ready(c), LOWS[c])
                        take_bank(k)
                        three(proj[k % 2][:, :], [(weight(c, 4 * (t % 2) + q), (o_hi[b % 2][:, q, :], o_lo[b % 2][:, q, :]))
                                                  for q in range(PAIRS)]).then_inc(full, 1)

                    def scores(pieces, banks, keys, queries, masks):
                        for n, (j, q0, w, b, col) in enumerate(pieces):
                            to, off = banks[b]
                            mm = three(to[:, off + col:off + col + w], [(keys(j), queries(q0, w))],
                                       start=off + col == 0)
                            for i, m in enumerate(masks[:w // P]):
                                mm = add(to[:, off + col + i * P:off + col + (i + 1) * P], cst[:, m, :],
                                         cst[:, IDENT, :])
                            if n + 1 == len(pieces) or pieces[n + 1][3] != b:
                                mm.then_inc(score_full, 1)

                    def values(n, pieces, vals):
                        pe.wait_ge(p_l, n + 1)
                        if n:
                            pe.wait_ge(pv_free, n)
                        for i, (j, q0, w, b, col) in enumerate(pieces):
                            if pieces is BANDED:
                                s = slice(q0 * 2, q0 * 2 + w)
                                probs = bp_hi[:, s], bp_lo[:, s]
                            else:
                                s = slice(b * SEQ + col, b * SEQ + col + w)
                                probs = p_hi[:, s], p_lo[:, s]
                            mm = three(pv_bank[:, q0:q0 + w], [(vals(j), probs)], start=i == 0)
                        mm.then_inc(pv_full, 1)

                    norm_sum(PRE)
                    two_tiles(("latent", 0), ("latent", 1), h_hi, h_lo, hlo)
                    tile(("latent", 2), h_hi, h_lo)
                    norm_sum(QLAT)
                    tile(("latent", 3), h_hi, h_lo)
                    norm_sum(KVLAT)
                    tile(("gate", 0, 0), h_hi, h_lo)

                    def mla_qk(h):
                        c, k = C["mla", h], T["mla_q", h]
                        pe.wait_ge(low_ready(c), LOWS[c])
                        pe.wait_ge(hlo, 11)
                        take_bank(k)
                        three(proj[k % 2][:, :], [(weight(c, t), (cqn_hi[:, t, :], cqn_lo[:, t, :]))
                                                  for t in range(2)]).then_inc(full, 1)
                        assert T["mla_k", h] == k + 1
                        take_bank(k + 1)
                        three(proj[(k + 1) % 2][:, :], [(weight(c, 2), (ckn_hi[:, :], ckn_lo[:, :]))])\
                            .then_inc(full, 1)

                    def mla_v(h):
                        c, k = C["mla", h], T["mla_v", h]
                        take_bank(k)
                        whi_, wlo_ = weight(c, 2)
                        for j in range(NB):
                            tok = slice(j * P, (j + 1) * P)
                            mm = three(proj[k % 2][:, j * HEAD:(j + 1) * HEAD],
                                       [((ckn_hi[:, tok], ckn_lo[:, tok]), (whi_[:, HEAD:P], wlo_[:, HEAD:P]))],
                                       start=j == 0)
                        mm.then_inc(full, 1)

                    def mla_scores(h):
                        s = h % 2
                        pe.wait_ge(mq_l, h + 1)
                        k = T["mla_k", h]
                        pe.wait_ge(free[k % 2], k // 2 + 1)
                        if h == 0:
                            pe.wait_ge(kr_lo, 2)
                        else:
                            pe.wait_ge(score_free, h)
                        scores(CAUSAL, [(b, 0) for b in score],
                               lambda j: (mk_hi[:, s, j * P:(j + 1) * P], mk_lo[:, s, j * P:(j + 1) * P]),
                               lambda q0, w: (mq_hi[:, s, q0:q0 + w], mq_lo[:, s, q0:q0 + w]), [MASK_CAUSAL])

                    def mla_values(h):
                        s = h % 2
                        k = T["mla_v", h]
                        pe.wait_ge(free[k % 2], k // 2 + 1)
                        if h == 0:
                            pe.wait_ge(ones_set, 2)
                        values(h, CAUSAL, lambda j: (mv_hi[:, s, j, :], mv_lo[:, s, j, :]))

                    mla_qk(0)
                    mla_v(0)
                    mla_scores(0)
                    tile(("gate", 0, 1), h_hi, h_lo)
                    mla_qk(1)
                    mla_v(1)
                    for h in range(HEADS):
                        if h + 1 < HEADS:
                            mla_scores(h + 1)
                        if h + 2 < HEADS:
                            mla_qk(h + 2)
                        mla_values(h)
                        if h == HEADS - 2:
                            tile(("swa_k",), h_hi, h_lo)
                            tile(("swa_vt",), h_hi, h_lo)
                        if h + 2 < HEADS:
                            mla_v(h + 2)
                            tile(("gate", 0, h + 2), h_hi, h_lo)

                    def rotate(n):
                        pe.wait_ge(rp_l, n + 1)
                        if n:
                            pe.wait_ge(rot_used, n)
                        pe.matmul(rot_bank[:, :], cst[:, SWAP, :], rp_hi[:, :], start=True, stop=False)
                        pe.matmul(rot_bank[:, :], cst[:, SWAP, :], rp_lo[:, :], start=False, stop=True)\
                          .then_inc(rot, 1)

                    def band_scores(n):
                        t, r = n // 2, n % 2
                        rows = slice(HEAD * r, HEAD * (r + 1))
                        pe.wait_ge(rpo_l, t + 2)
                        if n == 1:
                            pe.wait_ge(rot_used, PAIRS + 1)
                        pe.wait_ge(score_free, HEADS + max(n - 1, 0))
                        scores(BANDED, [(b, 0) for b in band[r]],
                               lambda j: (wk_hi[rows, j * P:(j + 1) * P], wk_lo[rows, j * P:(j + 1) * P]),
                               lambda q0, w: (wq_hi[rows, t, q0:q0 + w], wq_lo[rows, t, q0:q0 + w]),
                               [MASK_CAUSAL, MASK_PREV])

                    rotate(0)
                    tile(("swa_q", 0), h_hi, h_lo)
                    turn(("swa_v",), 1, vt_at(None))
                    tile(("swa_q", 1), h_hi, h_lo)
                    rotate(1)
                    tile(("swa_q", 2), h_hi, h_lo)
                    rotate(2)
                    band_scores(0)
                    tile(("swa_q", 3), h_hi, h_lo)
                    rotate(3)
                    tile(("stick", 0, 0), h_hi, h_lo)
                    rotate(4)
                    tile(("stick", 0, 1), h_hi, h_lo)
                    band_scores(1)
                    k = T["swa_v",]
                    pe.wait_ge(free[k % 2], k // 2 + 1)
                    pe.wait_ge(ones_set, 4)
                    for n in range(HEADS):
                        if n + 2 < HEADS:
                            band_scores(n + 2)
                        if n:
                            out_tile(0, n)
                        if n == HEADS - 1:
                            tile(("stick_vt", 0), h_hi, h_lo)
                        values(HEADS + n, BANDED, lambda j: (wv_hi[:, j, n % 2, :], wv_lo[:, j, n % 2, :]))
                        if n == 0:
                            pe.wait_ge(o_l, PAIRS)
                            out_tile(0, 0)

                    def stick_scores(p):
                        for i in range(2):
                            k = T["stick", p, i]
                            pe.wait_ge(free[k % 2], k // 2 + 1)
                        if p:
                            pe.wait_ge(a_exp, 6 * p)
                        else:
                            pe.wait_ge(score_free, 2 * HEADS)

                        def piece(r, n):
                            j, q0, w, b, col = CAUSAL[n]
                            rows = slice(HEAD * r, HEAD * (r + 1))
                            to, off = stick[r][b]
                            key, query = slice(j * P, (j + 1) * P), slice(q0, q0 + w)
                            return three(to[:, off + col:off + col + w],
                                         [((stick_in_hi(p, 1)[rows, key], stick_in_lo(p, 1)[rows, key]),
                                           (stick_in_hi(p, 0)[rows, query], stick_in_lo(p, 0)[rows, query]))],
                                         start=off + col == 0)

                        piece(0, 0).then_inc(score_full, 1)
                        piece(0, 1)
                        piece(0, 2).then_inc(score_full, 1)
                        piece(0, 3).then_inc(shared_half, 1)
                        pe.wait_ge(shared_half, p + 1)
                        piece(1, 3).then_inc(score_full, 1)
                        piece(1, 0).then_inc(score_full, 1)
                        piece(1, 1)
                        piece(1, 2).then_inc(score_full, 1)

                    def stick_tail(h):
                        pe.wait_ge(sp_l, h + 1)
                        for n, (j, q0, w, b, col) in enumerate(CAUSAL):
                            to, off = stick[h % 2][b]
                            if h % 2 and b == 2:
                                pe.wait_ge(a_exp, 3 * h)
                            for (j2, q2, w2, b2, col2) in CAUSAL:
                                if j2 < j:
                                    continue
                                m = NEG_TRI if j2 == j else NEG_ONE
                                o = to[:, off + col + q2 - q0:off + col + w]
                                s = slice(b2 * SEQ + col2, b2 * SEQ + col2 + w2)
                                add(o, cst[:, m, :], sp_hi[:, s])
                                add(o, cst[:, m, :], sp_lo[:, s])
                            mm = add(to[:, off + col:off + col + P], cst[:, MASK_STRICT, :], cst[:, IDENT, :])
                            if n != 1:
                                mm.then_inc(tail_full, 1)

                    def stick_values(h):
                        s, k = h // 2 % 2, T["stick", h // 2, 2]
                        pe.wait_ge(free[k % 2], k // 2 + 1)
                        values(2 * HEADS + h, CAUSAL,
                               lambda j: (sb_hi[s][:, 2, j * P:(j + 1) * P], sb_lo[s][:, 2, j * P:(j + 1) * P]))

                    turn(("stick", 0, 2), 2, vt_at(0))
                    stick_scores(0)
                    for p in range(PAIRS):
                        more = p + 1 < PAIRS
                        if more:
                            tile(("stick", p + 1, 0), h_hi, h_lo)
                            tile(("stick", p + 1, 1), h_hi, h_lo)
                        else:
                            tile(("gate", 2, 0), h_hi, h_lo)
                            tile(("gate", 2, 1), h_hi, h_lo)
                        stick_tail(2 * p)
                        if more:
                            tile(("stick_vt", p + 1), h_hi, h_lo)
                        else:
                            tile(("gate", 2, 2), h_hi, h_lo)
                        stick_tail(2 * p + 1)
                        stick_values(2 * p)
                        tile(("gate", 1, 2 * p), h_hi, h_lo)
                        if more:
                            turn(("stick", p + 1, 2), p + 3, vt_at(p + 1))
                        else:
                            tile(("gate", 2, 3), h_hi, h_lo)
                        tile(("gate", 1, 2 * p + 1), h_hi, h_lo)
                        if more:
                            stick_scores(p + 1)
                        if p == 0:
                            pe.wait_ge(o_l, 2 * PAIRS)
                        out_tile(1, 2 * p)
                        out_tile(1, 2 * p + 1)
                        stick_values(2 * p + 1)

                    for t in range(0, KT, 2):
                        if t > 3:
                            tile(("gate", 2, t), h_hi, h_lo)
                            tile(("gate", 2, t + 1), h_hi, h_lo)
                        if t == 0:
                            pe.wait_ge(pv_free, 3 * HEADS)
                        out_tile(2, t)
                        out_tile(2, t + 1)

                    for t in range(KT):
                        tile(("out", t), mix_hi, mix_lo, (mix_l, 0) if t == 0 else None)
                    norm_sum(POST)
                    def up(g):
                        if g == 0:
                            two_tiles(("up", 0, 0), ("up", 0, 1), h_hi, h_lo, xg_lo)
                        for t in range(0 if g else 2, KT):
                            if g == 1 and t == 3:
                                norm_sum(MPRE)
                            tile(("up", g, t), h_hi, h_lo)

                    def down(g):
                        for t in range(KT):
                            tile(("down", g, t), u_hi[g % 2], u_lo[g % 2], (u_l, KT * g) if t == 0 else None)

                    up(0)
                    for g in range(GROUPS):
                        if g + 1 < GROUPS:
                            up(g + 1)
                        down(g)
                    norm_sum(MPOST)

                @block.scalar
                def _(act):
                    LN_EXP = "natural_log_exp_and_others"

                    def split(c):
                        if c >= CHUNKS:
                            return
                        n = c // RING + 1
                        act.wait_ge(loaded[c % RING], 16 * (c // RING + 1))
                        if c >= RING:
                            act.wait_ge(full, LAST[c - RING] + 1)
                        w = WIDTH[c]
                        act.activation(w_hi[:, c % RING, 0:w], raw[:, c % RING, 0:w], ACT.Copy).then_inc(whi, 1)

                    def square(n, src, after=None):
                        if after:
                            act.wait_ge(after[0], after[1])
                        if n > 1:
                            act.wait_ge(summed, n - 1)
                        act.activation(sq[:, n % 2, :], src, ACT.Square).then_inc(squared, 1)

                    def norm_guess(nu, width):
                        act.wait_ge(sum_all, nu + 1)
                        act.activation(rs0[:, :], norm_bank[:, :], ACT.Ln, bias=EPS, scale=1.0 / width)\
                           .then_inc(rs_guess, 1)
                        act.wait_ge(rs_guess, 2 * nu + 1)
                        act.activation(rs0[:, :], rs0[:, :], ACT.Exp, scale=-0.5).then_inc(rs_guess, 1)

                    def norm_hi(nu, n, dst):
                        act.wait_ge(hf_set, n + 1)
                        act.activation(dst, hf[:, n % 2, :], ACT.Copy).then_inc(hhi, 1)

                    def tile_ready(k):
                        act.wait_ge(full, k + 1)

                    def soft_out(n):
                        if n < HEADS:
                            act.wait_ge(pv_full, n + 1)
                            src = pv_bank[HEAD:P, :]
                        else:
                            act.wait_ge(den, n - HEADS + 1)
                            src = dn[HEAD:P, :]
                        if n > 0:
                            act.wait_ge(pv_free, n)
                        act.activation(dn[0:HEAD, :], src, ACT.Ln).then_inc(den_inv, 1)
                        act.wait_ge(den_inv, 2 * n + 1)
                        act.activation(dn[0:HEAD, :], dn[0:HEAD, :], ACT.Exp, scale=-1.0).then_inc(den_inv, 1)

                    def out_hi(n):
                        b, q = n // 2 // PAIRS, n // 2 % PAIRS
                        act.wait_ge(pv_free, n + 1)
                        act.activation(o_hi[b][:, q, :], of[:, :], ACT.Copy).then_inc(o_h, 1)

                    def soft_exp(n, src, scale):
                        act.wait_ge(sub, n + 1)
                        act.activation(src, src, ACT.Exp, scale=scale).then_inc(p_exp, 1)

                    def soft_hi(n, src, dst):
                        act.wait_ge(p_exp, n + 1)
                        if n > 0:
                            act.wait_ge(pv_full, n)
                        act.activation(dst, src, ACT.Copy).then_inc(p_h, 1)

                    act.preload_act_table_set(LN_EXP)
                    for t in range(KT):
                        square(t, x[:, t, :])
                    split(0)
                    split(1)
                    norm_guess(PRE, D)
                    for t in range(KT):
                        norm_hi(PRE, t, h_hi[:, t, :])
                    def latent(i):
                        split(i + 2)
                        tile_ready(i)
                        act.activation(cf[:, i, :], proj[i % 2][:, :], ACT.Copy).then_inc(free[i % 2], 1)

                    latent(0)
                    latent(1)
                    for i in range(2):
                        square(SQ0[QLAT] + i, cf[:, i, :], (free[i % 2], 1))
                    latent(2)
                    square(SQ0[KVLAT], cf[:, 2, :], (free[0], 2))
                    norm_guess(QLAT, Q_LORA)
                    for i in range(2):
                        norm_hi(QLAT, 8 + i, cqn_hi[:, i, :])
                    split(3 + 2)
                    norm_guess(KVLAT, KV_LORA)
                    norm_hi(KVLAT, 10, ckn_hi[:, :])
                    for s in range(2):
                        act.wait_ge(kr_sum, 1)
                        act.activation(mk_hi[HEAD:P, s, :], ra[HEAD:P, :], ACT.Copy).then_inc(kr_hi, 1)

                    def gate_a(t):
                        k = T["gate", 0, t]
                        tile_ready(k)
                        act.activation(mix[:, t, :], proj[k % 2][:, :], ACT.Identity,
                                       bias=vec[:, V_GATE + t:V_GATE + t + 1]).then_inc(free[k % 2], 1)

                    def mla_qk(h):
                        k, s = T["mla_q", h], h % 2
                        act.wait_ge(mq_f, h + 1)
                        act.activation(mq_hi[:, s, :], mqf[:, :], ACT.Copy).then_inc(mq_h, 1)
                        tile_ready(k + 1)
                        act.activation(mk_hi[0:HEAD, s, :], proj[(k + 1) % 2][0:HEAD, :], ACT.Copy)\
                           .then_inc(mk_h, 1)
                        split(C["mla", h] + 2)

                    def mla_v(h):
                        k, s = T["mla_v", h], h % 2
                        tile_ready(k)
                        act.activation(mv_hi[:, s, :, 0:HEAD],
                                       proj[k % 2][:, 0:NB * HEAD].rearrange("p (j d) -> p j d", j=NB), ACT.Copy)\
                           .then_inc(mv_h, 1)

                    for h in range(2):
                        split(C["gate", 0, h] + 2)
                        gate_a(h)
                        mla_qk(h)
                        mla_v(h)
                    for h in range(HEADS):
                        soft_exp(h, s_f[:, :], float((HEAD + ROPE_DIM) ** -0.5))
                        soft_hi(h, s_f[:, :], p_hi[:, :])
                        if h == HEADS - 1:
                            split(C["swa_k",] + 2)
                        if 1 <= h < HEADS - 1:
                            gate_a(h + 1)
                        if h == HEADS - 2:
                            act.wait_ge(free[T["gate", 0, KT - 1] % 2], T["gate", 0, KT - 1] // 2 + 1)
                            act.wait_ge(free[T["gate", 0, KT - 2] % 2], T["gate", 0, KT - 2] // 2 + 1)
                            act.activation(mix[:, :, :], mix[:, :, :], ACT.Sigmoid).then_inc(mix_gate, 1)
                            act.preload_act_table_set(LN_EXP)
                        if h + 2 < HEADS:
                            mla_qk(h + 2)
                        soft_out(h)
                        if h + 2 < HEADS:
                            mla_v(h + 2)
                            split(C["gate", 0, h + 2] + 2)
                        if h % 2:
                            out_hi(h)

                    def rope(n, k, scale, dst):
                        tile_ready(k)
                        if n:
                            act.wait_ge(rot, n)
                        act.activation(rp_hi[:, :], proj[k % 2][:, :], ACT.Copy, scale=scale).then_inc(rp_h, 1)

                    def rope_out(n, dst):
                        act.wait_ge(rp_sum, n + 1)
                        act.activation(dst, ra[:, :], ACT.Copy).then_inc(rpo_h, 1)

                    rope(0, T["swa_k",], 1.0, None)
                    rope_out(0, wk_hi[:, :])
                    def turned_in(n, name, src):
                        k = T[name]
                        split(C[name] + 2)
                        tile_ready(k)
                        act.activation(src, proj[k % 2][:, :], ACT.Copy).then_inc(vt_set, 1)
                        act.wait_ge(vt_set, n)
                        act.sem_inc(free[k % 2], 1)

                    turned_in(1, ("swa_vt",), vt_at(None))
                    for t in range(PAIRS):
                        split(C["swa_q", t] + 2)
                        rope(t + 1, T["swa_q", t], 0.125, None)
                        if t == 0:
                            k = T["swa_v",]
                            tile_ready(k)
                            act.activation(wv_hi[:, :, :, 0:HEAD], proj[k % 2][:, :].rearrange("p (j v d) -> p j v d", j=NB, v=2),
                                           ACT.Copy).then_inc(wv_h, 1)
                        rope_out(t + 1, wq_hi[:, t, :])

                    def stick_in(p, i):
                        name = ("stick", p, i)
                        k = T[name]
                        if i < 2:
                            split(C[name] + 2)
                        tile_ready(k)
                        act.activation(stick_in_hi(p, i), proj[k % 2][:, :], ACT.Copy, scale=0.125 if i == 0 else 1.0)\
                           .then_inc(sbh, 1)

                    stick_in(0, 0)
                    stick_in(0, 1)
                    for n in range(HEADS + 1):
                        if n < HEADS:
                            soft_exp(HEADS + n, bs_f[:, :], 1.0)
                            soft_hi(HEADS + n, bs_f[:, :], bp_hi[:, :])
                        if n:
                            soft_out(HEADS + n - 1)
                        if n < HEADS:
                            head = n // 2 + 4 * (n % 2)
                            act.wait_ge(mx_sink, n + 1)
                            act.wait_ge(den_inv, 2 * (HEADS + n) - 1)
                            act.activation(dn[HEAD:P, :], bmxr[n % 2][HEAD:P, :], ACT.Exp, scale=-1.0,
                                           bias=vec[HEAD:P, V_SINK + head:V_SINK + head + 1]).then_inc(sink_e, 1)
                        if n and n % 2 == 0:
                            out_hi(HEADS + n - 1)
                        if n < HEADS:
                            if n % 2 == 0:
                                split(C["o", 0, n // 2] + 2)
                            if n == HEADS - 1:
                                turned_in(2, ("stick_vt", 0), vt_at(0))

                    def stick_ln(h):
                        b = fb[h % 2][:, :]
                        act.wait_ge(z_exp, h + 1)
                        act.activation(b, b, ACT.Ln, bias=1.0).then_inc(z_ln, 1)

                    def stick_exp(h):
                        b = fb[h % 2][:, :]
                        act.wait_ge(z_min, 3 * h + 3)
                        act.activation(b, b, ACT.Exp).then_inc(z_exp, 1)

                    def stick_hi(h):
                        act.wait_ge(z_mask, 4 * h + 4)
                        if h > 0:
                            act.wait_ge(tail_full, 3 * h)
                        act.activation(sp_hi[:, :], fb[h % 2][:, :], ACT.Copy).then_inc(sp_h, 1)

                    def stick_probs(h):
                        act.wait_ge(sp_l, h + 1)
                        for b, w in enumerate(STICK_COLS):
                            act.wait_ge(tail_full, 3 * h + b + 1)
                            src, off = stick[h % 2][b]
                            act.activation(fb[h % 2][:, b * SEQ:b * SEQ + w], src[:, off:off + w], ACT.Exp)\
                               .then_inc(a_exp, 1)

                    def stick_probs_hi(h):
                        act.wait_ge(a_exp, 3 * h + 3)
                        act.wait_ge(pv_full, 2 * HEADS + h)
                        act.activation(p_hi[:, :], fb[h % 2][:, :], ACT.Copy).then_inc(p_h, 1)

                    def stick_out(h):
                        rows = slice(HEAD * (h % 2), HEAD * (h % 2 + 1))
                        act.wait_ge(pv_full, 2 * HEADS + h + 1)
                        act.activation(o_hi[0][rows, h // 2, :], pv_bank[rows, :], ACT.Copy).then_inc(sbo_h, 1)

                    def gate_in_tile(t):
                        k = T["gate", 1, t]
                        split(C["gate", 1, t] + 2)
                        tile_ready(k)
                        if t > 1:
                            act.wait_ge(mix_add, t - 1)
                        act.activation(gate[:, t % 2, :], proj[k % 2][:, :], ACT.Identity,
                                       bias=vec[:, V_GATE + KT + t:V_GATE + KT + t + 1]).then_inc(gate_in, 1)
                        act.wait_ge(gate_in, t + 1)
                        act.sem_inc(free[k % 2], 1)

                    def gate2_tile(t):
                        k = T["gate", 2, t]
                        split(C["gate", 2, t] + 2)
                        tile_ready(k)
                        act.activation(gate2[:, t, :], proj[k % 2][:, :], ACT.Identity,
                                       bias=vec[:, V_GATE + 2 * KT + t:V_GATE + 2 * KT + t + 1]).then_inc(gate2_in, 1)
                        act.wait_ge(gate2_in, t + 1)
                        act.sem_inc(free[k % 2], 1)

                    stick_in(0, 2)
                    for p in range(PAIRS):
                        h, more = 2 * p, p + 1 < PAIRS
                        stick_exp(h)
                        stick_ln(h)
                        stick_exp(h + 1)
                        stick_ln(h + 1)
                        if p:
                            stick_out(h - 1)
                        if more:
                            stick_in(p + 1, 0)
                        else:
                            gate2_tile(0)
                        stick_hi(h)
                        if more:
                            stick_in(p + 1, 1)
                        else:
                            gate2_tile(1)
                        stick_hi(h + 1)
                        stick_probs(h)
                        stick_probs_hi(h)
                        if more:
                            turned_in(p + 3, ("stick_vt", p + 1), vt_at(p + 1))
                        else:
                            gate2_tile(2)
                        stick_probs(h + 1)
                        stick_out(h)
                        stick_probs_hi(h + 1)
                        gate_in_tile(2 * p)
                        if more:
                            stick_in(p + 1, 2)
                        else:
                            gate2_tile(3)
                        gate_in_tile(2 * p + 1)
                        split(C["o", 1, p] + 2)
                        act.activation(gate[:, :, :], gate[:, :, :], ACT.Sigmoid).then_inc(gate_set, 1)
                        if not more:
                            act.activation(gate2[:, :, :], gate2[:, :, :], ACT.Sigmoid).then_inc(gate_c, 1)
                        act.preload_act_table_set(LN_EXP)
                    stick_out(HEADS - 1)

                    def mix_high(t):
                        act.wait_ge(mix_add, KT + t + 1)
                        act.activation(mix_hi[:, t, :], mix[:, t, :], ACT.Copy).then_inc(mix_h, 1)

                    split(C["o", 2, 0] + 2)
                    mix_high(0)
                    mix_high(1)
                    split(C["o", 2, 1] + 2)
                    for t in range(4, KT):
                        k = T["gate", 2, t]
                        split(C["gate", 2, t] + 2)
                        tile_ready(k)
                        act.wait_ge(mix_add, KT + t - 1)
                        act.activation(gate[:, t % 2, :], proj[k % 2][:, :], ACT.Sigmoid,
                                       bias=vec[:, V_GATE + 2 * KT + t:V_GATE + 2 * KT + t + 1]).then_inc(gate_c, 1)
                        act.wait_ge(gate_c, t - 2)
                        act.sem_inc(free[k % 2], 1)
                        if t % 2:
                            split(C["o", 2, t // 2] + 2)
                            mix_high(t - 3)
                            mix_high(t - 2)
                    mix_high(KT - 2)
                    mix_high(KT - 1)
                    act.preload_act_table_set(LN_EXP)

                    for t in range(KT):
                        k = T["out", t]
                        split(C["out", t] + 2)
                        tile_ready(k)
                        act.activation(y[:, t, :], proj[k % 2][:, :], ACT.Copy).then_inc(free[k % 2], 1)
                        square(SQ0[POST] + t, y[:, t, :], (free[k % 2], k // 2 + 1))
                    norm_guess(POST, D)
                    for t in range(KT):
                        act.wait_ge(res, t + 1)
                        act.activation(h_hi[:, t, :], x[:, t, :], ACT.Copy, scale=vec[:, V_MPRE + t:V_MPRE + t + 1])\
                           .then_inc(xg_hi, 1)

                    def up(g):
                        for t in range(KT):
                            k, n = T["up", g, t], KT * g + t
                            split(C["up", g, t] + 2)
                            if g == 1 and t == 4:
                                norm_guess(MPRE, D)
                            tile_ready(k)
                            if n > 1:
                                act.wait_ge(u_s, n - 1)
                                act.wait_ge(u_h, n - 1)
                            act.activation(relu[:, n % 2, :], proj[k % 2][:, :], ACT.Relu).then_inc(free[k % 2], 1)
                            act.wait_ge(free[k % 2], k // 2 + 1)
                            act.activation(u_hi[g % 2][:, t, :], relu[:, n % 2, :], ACT.Square).then_inc(u_h, 1)
                            if g == 0:
                                square(SQ0[MPRE] + t, x[:, t, :])

                    def down(g):
                        for t in range(KT):
                            k = T["down", g, t]
                            split(C["down", g, t] + 2)
                            if g == GROUPS - 1:
                                square(SQ0[MPOST] + t, y[:, t, :], (y_set, t + 1))

                    up(0)
                    for g in range(GROUPS):
                        if g + 1 < GROUPS:
                            up(g + 1)
                        down(g)
                    norm_guess(MPOST, D)

                @block.vector
                def _(dve):
                    def split(c):
                        if c >= CHUNKS or BY_GPSIMD[c]:
                            return
                        dve.wait_ge(whi, c + 1)
                        w = WIDTH[c]
                        dve.tensor_tensor(w_lo[:, c % RING, 0:w], raw[:, c % RING, 0:w],
                                          w_hi[:, c % RING, 0:w].bitcast(F32), ALU.subtract).then_inc(wlo, 1)

                    def gather(nu, tiles, n0):
                        for i in range(tiles):
                            n = n0 + i
                            dve.wait_ge(squared, n + 1)
                            if i == 0:
                                if nu:
                                    dve.wait_ge(sum_split, 2 * nu)
                                dve.tensor_copy(acc[:, :], sq[:, n % 2, :]).then_inc(summed, 1)
                            else:
                                dve.wait_ge(summed, n)
                                dve.tensor_tensor(acc[:, :], acc[:, :], sq[:, n % 2, :], ALU.add).then_inc(summed, 1)

                    def norm_split(nu, width):
                        dve.wait_ge(summed, SQ0[nu + 1])
                        if nu:
                            dve.wait_ge(sum_all, nu)
                        dve.tensor_copy(acc_hi[:, :], acc[:, :]).then_inc(sum_split, 1)
                        dve.wait_ge(sum_split, 2 * nu + 1)
                        dve.tensor_tensor(acc_lo[:, :], acc[:, :], acc_hi[:, :].bitcast(F32), ALU.subtract)\
                           .then_inc(sum_split, 1)

                    def norm_refine(nu, width):
                        dve.wait_ge(rs_guess, 2 * nu + 1)
                        dve.tensor_scalar(ms[:, :], norm_bank[:, :], 1.0 / width, EPS, ALU.mult, ALU.add)\
                           .then_inc(rs_step, 1)
                        dve.wait_ge(rs_guess, 2 * nu + 2)
                        dve.tensor_tensor(rst[:, :], rs0[:, :], rs0[:, :], ALU.mult).then_inc(rs_step, 1)
                        dve.wait_ge(rs_step, 4 * nu + 2)
                        dve.scalar_tensor_tensor(out=rst[:, :], in0=rst[:, :], scalar=-0.5, in1=ms[:, :],
                                                 op0=ALU.mult, op1=ALU.mult).then_inc(rs_step, 1)
                        dve.wait_ge(rs_step, 4 * nu + 3)
                        dve.scalar_tensor_tensor(out=rstd[:, :], in0=rst[:, :], scalar=1.5, in1=rs0[:, :],
                                                 op0=ALU.add, op1=ALU.mult).then_inc(rs_step, 1)
                        dve.wait_ge(rs_step, 4 * nu + 4)

                    def normalize(n0, tiles, src, gain, his, los):
                        def scaled(i):
                            n = n0 + i
                            if n > 1:
                                dve.wait_ge(hlo, n - 1)
                            dve.scalar_tensor_tensor(out=hf[:, n % 2, :], in0=src(i), scalar=vec[:, gain + i:gain + i + 1],
                                                     in1=rstd[:, :], op0=ALU.mult, op1=ALU.mult).then_inc(hf_set, 1)

                        scaled(0)
                        for i in range(tiles):
                            n = n0 + i
                            if i + 1 < tiles:
                                scaled(i + 1)
                            dve.wait_ge(hhi, n + 1)
                            dve.tensor_tensor(los(i), hf[:, n % 2, :], his(i).bitcast(F32), ALU.subtract)\
                               .then_inc(hlo, 1)

                    def scaled(n, t, gain):
                        dve.scalar_tensor_tensor(out=hf[:, n % 3, :], in0=y[:, t, :], scalar=vec[:, gain + t:gain + t + 1],
                                                 in1=rstd[:, :], op0=ALU.mult, op1=ALU.mult).then_inc(scaled_y, 1)

                    def tile_ready(k):
                        dve.wait_ge(full, k + 1)

                    def low(k, dst, src, hi, after, scale=1.0):
                        dve.wait_ge(after[0], after[1])
                        if scale == 1.0:
                            ins = dve.tensor_tensor(dst, src, hi.bitcast(F32), ALU.subtract)
                        else:
                            ins = dve.scalar_tensor_tensor(out=dst, in0=src, scalar=scale, in1=hi.bitcast(F32),
                                                           op0=ALU.mult, op1=ALU.subtract)
                        ins.then_inc(free[k % 2], 1)

                    def probs_lo(n, src, hi, lo):
                        dve.wait_ge(p_h, n + 1)
                        dve.tensor_tensor(lo, src, hi.bitcast(F32), ALU.subtract).then_inc(p_l, 1)

                    def biggest(n, base, order, banks, to):
                        m = 4 * n
                        banded = order is not CAUSAL
                        last = n - 1 if banded and n > HEADS else n
                        if last > 0:
                            dve.wait_ge(mx_all, last)
                        for i, (j, q0, w, b, col) in enumerate(order):
                            dve.wait_ge(score_full, base + b + 1)
                            if i:
                                dve.wait_ge(mx_step, m + i)
                            src = banks[b][:, col:col + w]
                            if i == 0 or (banded and i == 1):
                                ins = dve.tensor_copy(to[:, q0:q0 + w], src)
                            else:
                                ins = dve.tensor_tensor(to[:, q0:q0 + w], src, to[:, q0:q0 + w], ALU.max)
                            ins.then_inc(mx_step, 1)

                    def subtract(n, pieces, banks, to, biggest_):
                        if n > 0:
                            dve.wait_ge(p_l, n)
                        for i, (j, q0, w, b, col) in enumerate(pieces):
                            s0 = b * SEQ + col if pieces is CAUSAL else 2 * q0
                            ins = dve.tensor_tensor(to[:, s0:s0 + w], banks[b][:, col:col + w],
                                                    biggest_[:, q0:q0 + w], ALU.subtract)
                        ins.then_inc(sub, 1)
                        dve.wait_ge(sub, n + 1)
                        dve.sem_inc(score_free, 1)

                    def soft_out(n):
                        dve.wait_ge(den_inv, 2 * n + 2)
                        rows = slice(HEAD * (n % 2), HEAD * (n % 2 + 1))
                        if n > 1:
                            dve.wait_ge(o_l, n // 2)
                        dve.tensor_tensor(of[rows, :], pv_bank[0:HEAD, :], dn[0:HEAD, :], ALU.mult)\
                           .then_inc(pv_free, 1)

                    def out_lo(n):
                        m = n // 2
                        b, q = m // PAIRS, m % PAIRS
                        dve.wait_ge(o_h, m + 1)
                        dve.tensor_tensor(o_lo[b][:, q, :], of[:, :], o_hi[b][:, q, :].bitcast(F32), ALU.subtract)\
                           .then_inc(o_l, 1)

                    dve.tensor_copy(vec[:, :], vec_all[:, bass.ds(l * VECS, VECS)]).then_inc(vec_set, 1)
                    dve.wait_ge(vec_set, 1)
                    gather(PRE, KT, 0)
                    norm_split(PRE, D)
                    split(0)
                    split(1)
                    norm_refine(PRE, D)
                    normalize(0, KT, lambda i: x[:, i, :], V_PRE, lambda i: h_hi[:, i, :], lambda i: h_lo[:, i, :])
                    split(2)
                    split(3)
                    gather(QLAT, 2, SQ0[QLAT])
                    norm_split(QLAT, Q_LORA)
                    split(4)
                    gather(KVLAT, 1, SQ0[KVLAT])
                    norm_refine(QLAT, Q_LORA)
                    normalize(8, 2, lambda i: cf[:, i, :], V_Q, lambda i: cqn_hi[:, i, :], lambda i: cqn_lo[:, i, :])
                    norm_split(KVLAT, KV_LORA)
                    tile_ready(3)
                    dve.tensor_tensor(ra[HEAD:P, :], proj[1][0:HEAD, :], KCOS[HEAD:P, :], ALU.mult)\
                       .then_inc(kr_part, 1)
                    dve.tensor_tensor(rb[HEAD:P, :], proj[1][HEAD:P, :], KSIN[HEAD:P, :], ALU.mult)\
                       .then_inc(free[1], 1)
                    split(5)
                    dve.wait_ge(kr_part, 1)
                    dve.wait_ge(free[1], 2)
                    dve.tensor_tensor(ra[HEAD:P, :], ra[HEAD:P, :], rb[HEAD:P, :], ALU.add).then_inc(kr_sum, 1)
                    norm_refine(KVLAT, KV_LORA)
                    normalize(10, 1, lambda i: cf[:, 2, :], V_KV, lambda i: ckn_hi[:, :], lambda i: ckn_lo[:, :])
                    split(C["gate", 0, 0] + 2)
                    for s in range(2):
                        dve.wait_ge(kr_hi, s + 1)
                        dve.tensor_tensor(mk_lo[HEAD:P, s, :], ra[HEAD:P, :], mk_hi[HEAD:P, s, :].bitcast(F32),
                                          ALU.subtract).then_inc(kr_lo, 1)

                    def mla_q(h):
                        k = T["mla_q", h]
                        tile_ready(k)
                        if h:
                            dve.wait_ge(mq_l, h)
                        dve.tensor_tensor(mqf[:, :], proj[k % 2][:, :], QPE, ALU.mult).then_inc(mq_f, 1)
                        dve.wait_ge(mq_f, h + 1)
                        dve.sem_inc(free[k % 2], 1)

                    def mla_qk(h):
                        k, s = T["mla_q", h], h % 2
                        dve.wait_ge(mq_h, h + 1)
                        dve.tensor_tensor(mq_lo[:, s, :], mqf[:, :], mq_hi[:, s, :].bitcast(F32), ALU.subtract)\
                           .then_inc(mq_l, 1)
                        low(k + 1, mk_lo[0:HEAD, s, :], proj[(k + 1) % 2][0:HEAD, :], mk_hi[0:HEAD, s, :], (mk_h, h + 1))
                        split(C["mla", h] + 2)

                    def mla_v(h):
                        k, s = T["mla_v", h], h % 2
                        low(k, mv_lo[:, s, :, 0:HEAD],
                            proj[k % 2][:, 0:NB * HEAD].rearrange("p (j d) -> p j d", j=NB), mv_hi[:, s, :, 0:HEAD],
                            (mv_h, h + 1))

                    def mla_biggest(h):
                        biggest(h, 3 * h, CAUSAL, score, mx)

                    def mla_subtract(h):
                        dve.wait_ge(mx_all, h + 1)
                        subtract(h, CAUSAL, score, s_f, mxr)

                    mla_q(0)
                    mla_qk(0)
                    mla_v(0)
                    mla_biggest(0)
                    split(C["gate", 0, 1] + 2)
                    mla_q(1)
                    mla_qk(1)
                    mla_v(1)
                    mla_subtract(0)
                    for h in range(HEADS):
                        probs_lo(h, s_f[:, :], p_hi[:, :], p_lo[:, :])
                        if h == HEADS - 1:
                            split(C["swa_k",] + 2)
                        if h + 1 < HEADS:
                            mla_biggest(h + 1)
                        if h + 2 < HEADS:
                            mla_q(h + 2)
                            mla_qk(h + 2)
                        if h + 1 < HEADS:
                            mla_subtract(h + 1)
                        soft_out(h)
                        if h + 2 < HEADS:
                            mla_v(h + 2)
                            split(C["gate", 0, h + 2] + 2)
                        if h % 2:
                            out_lo(h)

                    def rope_in(n, k, scale):
                        dve.wait_ge(rp_h, n + 1)
                        if n:
                            dve.wait_ge(rot, n)
                        if scale == 1.0:
                            dve.tensor_tensor(rp_lo[:, :], proj[k % 2][:, :], rp_hi[:, :].bitcast(F32), ALU.subtract)\
                               .then_inc(rp_l, 1)
                        else:
                            dve.scalar_tensor_tensor(out=rp_lo[:, :], in0=proj[k % 2][:, :], scalar=scale,
                                                     in1=rp_hi[:, :].bitcast(F32), op0=ALU.mult, op1=ALU.subtract)\
                               .then_inc(rp_l, 1)
                        if n:
                            dve.wait_ge(rpo_l, n)
                        dve.scalar_tensor_tensor(out=ra[:, :], in0=proj[k % 2][:, :], scalar=scale, in1=COS,
                                                 op0=ALU.mult, op1=ALU.mult).then_inc(free[k % 2], 1)

                    def rope_turn(n, k, dst, hi):
                        dve.wait_ge(rot, n + 1)
                        if n:
                            dve.wait_ge(rp_sum, n)
                        dve.tensor_tensor(rb[:, :], rot_bank[:, :], SIN, ALU.mult).then_inc(rot_used, 1)
                        dve.wait_ge(rot_used, n + 1)
                        dve.wait_ge(free[k % 2], k // 2 + 1)
                        dve.tensor_tensor(ra[:, :], ra[:, :], rb[:, :], ALU.add).then_inc(rp_sum, 1)
                        dve.wait_ge(rpo_h, n + 1)
                        dve.tensor_tensor(dst, ra[:, :], hi.bitcast(F32), ALU.subtract).then_inc(rpo_l, 1)

                    rope_in(0, T["swa_k",], 1.0)
                    rope_turn(0, T["swa_k",], wk_lo[:, :], wk_hi[:, :])
                    split(C["swa_vt",] + 2)
                    def band_biggest(n):
                        biggest(HEADS + n, 3 * HEADS + 2 * n, [BANDED[0], BANDED[2], BANDED[1], BANDED[3]], band[n % 2],
                                bmx[n % 2])

                    dve.wait_ge(pv_full, HEADS)
                    for t in range(PAIRS):
                        split(C["swa_q", t] + 2)
                        rope_in(t + 1, T["swa_q", t], 0.125)
                        if t == 0:
                            k = T["swa_v",]
                            low(k, wv_lo[:, :, :, 0:HEAD], proj[k % 2][:, :].rearrange("p (j v d) -> p j v d", j=NB, v=2),
                                wv_hi[:, :, :, 0:HEAD], (wv_h, 1))
                        rope_turn(t + 1, T["swa_q", t], wq_lo[:, t, :], wq_hi[:, t, :])
                        if t == 2:
                            band_biggest(0)

                    def stick_in(p, i):
                        name = ("stick", p, i)
                        if i < 2:
                            split(C[name] + 2)
                        low(T[name], stick_in_lo(p, i), proj[T[name] % 2][:, :], stick_in_hi(p, i), (sbh, 3 * p + i + 1),
                            0.125 if i == 0 else 1.0)

                    stick_in(0, 0)
                    stick_in(0, 1)
                    band_biggest(1)
                    for n in range(HEADS + 1):
                        if n < HEADS:
                            head = n // 2 + 4 * (n % 2)
                            dve.wait_ge(mx_all, HEADS + n + 1)
                            dve.tensor_scalar(bmxr[n % 2][:, :], bmxr[n % 2][:, :],
                                              vec[:, V_SINK + head:V_SINK + head + 1], None, ALU.max).then_inc(mx_sink, 1)
                            dve.wait_ge(mx_sink, n + 1)
                            subtract(HEADS + n, BANDED, band[n % 2], bs_f, bmxr[n % 2])
                        if n > 2 and n % 2:
                            out_lo(HEADS + n - 2)
                        if n % 2 and n < HEADS:
                            split(C["o", 0, n // 2] + 2)
                        if n:
                            dve.wait_ge(pv_full, HEADS + n)
                            dve.wait_ge(sink_e, n)
                            dve.tensor_tensor(dn[HEAD:P, :], pv_bank[HEAD:P, :], dn[HEAD:P, :], ALU.add)\
                               .then_inc(den, 1)
                            k = T["o", 0, n - 1]
                            tile_ready(k)
                            dve.wait_ge(mix_gate, 1)
                            dve.tensor_tensor(mix[:, n - 1, :], proj[k % 2][:, :], mix[:, n - 1, :], ALU.mult)\
                               .then_inc(free[k % 2], 1)
                        if n + 2 < HEADS:
                            band_biggest(n + 2)
                        if n:
                            soft_out(HEADS + n - 1)
                    out_lo(2 * HEADS - 1)

                    def stick_min(h):
                        for b, w in enumerate(STICK_COLS):
                            dve.wait_ge(score_full, 5 * HEADS + 5 * (h // 2) + (3 if b == 2 else b + 1 + 3 * (h % 2)))
                            if b == 0:
                                dve.wait_ge(p_l, 2 * HEADS + max(h - 1, 0))
                                if h < 2:
                                    dve.wait_ge(pv_full, 2 * HEADS)
                            src, off = stick[h % 2][b]
                            dve.tensor_scalar(fb[h % 2][:, b * SEQ:b * SEQ + w], src[:, off:off + w], 40.0, None, ALU.min)\
                               .then_inc(z_min, 1)

                    def stick_max(h):
                        dve.wait_ge(z_ln, h + 1)
                        for b, w in enumerate(STICK_COLS):
                            src, off = stick[h % 2][b]
                            to = fb[h % 2][:, b * SEQ:b * SEQ + w]
                            dve.tensor_tensor(to, src[:, off:off + w], to, ALU.max).then_inc(z_max, 1)

                    def stick_lo(h):
                        dve.wait_ge(sp_h, h + 1)
                        dve.tensor_tensor(sp_lo[:, :], fb[h % 2][:, :], sp_hi[:, :].bitcast(F32), ALU.subtract)\
                           .then_inc(sp_l, 1)

                    def stick_out(h):
                        rows = slice(HEAD * (h % 2), HEAD * (h % 2 + 1))
                        dve.wait_ge(sbo_h, h + 1)
                        dve.tensor_tensor(o_lo[0][rows, h // 2, :], pv_bank[rows, :], o_hi[0][rows, h // 2, :].bitcast(F32),
                                          ALU.subtract).then_inc(pv_free, 1)

                    def gated(b, t):
                        k = T["o", b, t]
                        tile_ready(k)
                        if b == 1:
                            dve.wait_ge(gate_set, t // 2 + 1)
                        else:
                            dve.wait_ge(gate_c, max(t - 2, 1))
                        g = gated_at(b, t)
                        dve.tensor_tensor(g, proj[k % 2][:, :], g, ALU.mult).then_inc(free[k % 2], 1)

                    split(C["stick_vt", 0] + 2)
                    stick_in(0, 2)
                    for p in range(PAIRS):
                        h, more = 2 * p, p + 1 < PAIRS
                        stick_min(h)
                        stick_min(h + 1)
                        if p:
                            gated(1, 2 * p - 2)
                            gated(1, 2 * p - 1)
                        stick_max(h)
                        if p:
                            stick_out(h - 1)
                        stick_max(h + 1)
                        if more:
                            stick_in(p + 1, 0)
                        else:
                            split(C["gate", 2, 0] + 2)
                        stick_lo(h)
                        if more:
                            stick_in(p + 1, 1)
                        else:
                            split(C["gate", 2, 1] + 2)
                        stick_lo(h + 1)
                        probs_lo(2 * HEADS + h, fb[0][:, :], p_hi[:, :], p_lo[:, :])
                        if more:
                            split(C["stick_vt", p + 1] + 2)
                        else:
                            split(C["gate", 2, 2] + 2)
                        stick_out(h)
                        probs_lo(2 * HEADS + h + 1, fb[1][:, :], p_hi[:, :], p_lo[:, :])
                        split(C["gate", 1, 2 * p] + 2)
                        if more:
                            stick_in(p + 1, 2)
                        else:
                            split(C["gate", 2, 3] + 2)
                        split(C["gate", 1, 2 * p + 1] + 2)
                        split(C["o", 1, p] + 2)
                    gated(1, KT - 2)
                    gated(1, KT - 1)
                    stick_out(HEADS - 1)

                    def mix_low(t):
                        dve.wait_ge(mix_h, t + 1)
                        dve.tensor_tensor(mix_lo[:, t, :], mix[:, t, :], mix_hi[:, t, :].bitcast(F32), ALU.subtract)\
                           .then_inc(mix_l, 1)

                    for t in range(0, KT, 2):
                        if t > 3:
                            split(C["gate", 2, t] + 2)
                            split(C["gate", 2, t + 1] + 2)
                        split(C["o", 2, t // 2] + 2)
                        if t:
                            mix_low(t - 2)
                            mix_low(t - 1)
                        gated(2, t)
                        gated(2, t + 1)
                    mix_low(KT - 2)
                    mix_low(KT - 1)

                    for t in range(KT):
                        split(C["out", t] + 2)
                        n = SQ0[POST] + t
                        dve.wait_ge(squared, n + 1)
                        if t == 0:
                            dve.tensor_copy(acc[:, :], sq[:, n % 2, :]).then_inc(summed, 1)
                        else:
                            dve.wait_ge(summed, n)
                            dve.tensor_tensor(acc[:, :], acc[:, :], sq[:, n % 2, :], ALU.add).then_inc(summed, 1)
                    norm_split(POST, D)
                    norm_refine(POST, D)
                    for t in range(KT + 2):
                        if t < KT:
                            if t > 2:
                                dve.wait_ge(res, t - 2)
                            scaled(t, t, V_POST)
                        if t > 1:
                            i = t - 2
                            dve.wait_ge(xg_hi, i + 1)
                            dve.scalar_tensor_tensor(out=h_lo[:, i, :], in0=x[:, i, :], scalar=vec[:, V_MPRE + i:V_MPRE + i + 1],
                                                     in1=h_hi[:, i, :].bitcast(F32), op0=ALU.mult,
                                                     op1=ALU.subtract).then_inc(xg_lo, 1)

                    def up(g):
                        for t in range(KT):
                            k, n = T["up", g, t], KT * g + t
                            split(C["up", g, t] + 2)
                            if g == 1 and t == 4:
                                norm_refine(MPRE, D)
                                dve.tensor_tensor(rsq[:, :], rstd[:, :], rstd[:, :], ALU.mult).then_inc(rsq_set, 1)
                            dve.wait_ge(free[k % 2], k // 2 + 1)
                            if n > 1:
                                dve.wait_ge(u_l, n - 1)
                            dve.tensor_tensor(usq[:, n % 2, :], relu[:, n % 2, :], relu[:, n % 2, :], ALU.mult)\
                               .then_inc(u_s, 1)
                            dve.wait_ge(u_h, n + 1)
                            dve.wait_ge(u_s, n + 1)
                            dve.tensor_tensor(u_lo[g % 2][:, t, :], usq[:, n % 2, :], u_hi[g % 2][:, t, :].bitcast(F32),
                                              ALU.subtract).then_inc(u_l, 1)
                            if g == 0:
                                n = SQ0[MPRE] + t
                                dve.wait_ge(squared, n + 1)
                                if t == 0:
                                    dve.tensor_copy(acc[:, :], sq[:, n % 2, :]).then_inc(summed, 1)
                                else:
                                    dve.wait_ge(summed, n)
                                    dve.tensor_tensor(acc[:, :], acc[:, :], sq[:, n % 2, :], ALU.add).then_inc(summed, 1)
                                if t == KT - 1:
                                    norm_split(MPRE, D)

                    def down(g):
                        for t in range(KT):
                            k = T["down", g, t]
                            split(C["down", g, t] + 2)
                            tile_ready(k)
                            if g == 0:
                                ins = dve.tensor_copy(y[:, t, :], proj[k % 2][:, :])
                            else:
                                last = T["down", g - 1, t]
                                dve.wait_ge(free[last % 2], last // 2 + 1)
                                ins = dve.tensor_tensor(y[:, t, :], proj[k % 2][:, :], y[:, t, :], ALU.add)
                            ins.then_inc(free[k % 2], 1)
                            if g == GROUPS - 1:
                                dve.wait_ge(free[k % 2], k // 2 + 1)
                                dve.wait_ge(rsq_set, 1)
                                dve.tensor_tensor(y[:, t, :], y[:, t, :], rsq[:, :], ALU.mult).then_inc(y_set, 1)
                                n = SQ0[MPOST] + t
                                dve.wait_ge(squared, n + 1)
                                if t == 0:
                                    dve.tensor_copy(acc[:, :], sq[:, n % 2, :]).then_inc(summed, 1)
                                else:
                                    dve.wait_ge(summed, n)
                                    dve.tensor_tensor(acc[:, :], acc[:, :], sq[:, n % 2, :], ALU.add).then_inc(summed, 1)

                    up(0)
                    for g in range(GROUPS):
                        if g + 1 < GROUPS:
                            up(g + 1)
                        down(g)
                    norm_split(MPOST, D)
                    norm_refine(MPOST, D)
                    for t in range(KT):
                        if t == 0:
                            dve.wait_ge(y_set, KT)
                        if t > 2 and t % 2 == 0:
                            dve.wait_ge(res, KT + (t - 2) // 2)
                        elif t > 2:
                            dve.wait_ge(res_even, (t - 1) // 2)
                        n = KT + t
                        scaled(n + 1, t, V_MPOST)
                        if t % 2 == 0:
                            dve.wait_ge(scaled_y, n + 1)
                            dve.tensor_tensor(x[:, t, :], x[:, t, :], hf[:, (n + 1) % 3, :], ALU.add).then_inc(res_even, 1)

                @block.gpsimd
                def _(pool):
                    pool.wait_ge(full, 1)
                    pool.memset(mv_hi[:, :, :, HEAD:P].bitcast(F32), 1.0).then_inc(ones_set, 1)
                    pool.memset(mv_lo[:, :, :, HEAD:P].bitcast(F32), 0.0).then_inc(ones_set, 1)
                    def split(*name):
                        c = C[name]
                        pool.wait_ge(whi, c + 1)
                        pool.tensor_tensor(w_lo[:, c % RING, :], raw[:, c % RING, :], w_hi[:, c % RING, :].bitcast(F32),
                                           ALU.subtract).then_inc(wlo_pool, 1)

                    for n in range(HEADS):
                        pool.wait_ge(mx_step, 4 * n + 4)
                        if n:
                            pool.wait_ge(score_free, n)
                        pool.partition_all_reduce(mxr[:, :], mx[:, :], P, bass.bass_isa.ReduceOp.max)\
                            .then_inc(mx_all, 1)
                        if n + 2 < HEADS:
                            split("gate", 0, n + 2)
                    pool.wait_ge(full, T["swa_q", 0] + 1)
                    pool.memset(wv_hi[:, :, :, HEAD:P].bitcast(F32), 1.0).then_inc(ones_set, 1)
                    pool.memset(wv_lo[:, :, :, HEAD:P].bitcast(F32), 0.0).then_inc(ones_set, 1)
                    def band_maximum(n):
                        pool.wait_ge(mx_step, 4 * n + 4)
                        if n > HEADS + 1:
                            pool.wait_ge(score_free, n - 1)
                            pool.wait_ge(sink_e, n - HEADS - 1)
                        pool.partition_all_reduce(bmxr[n % 2][:, :], bmx[n % 2][:, :], P, bass.bass_isa.ReduceOp.max)\
                            .then_inc(mx_all, 1)

                    band_maximum(HEADS)
                    band_maximum(HEADS + 1)
                    for n in range(HEADS, 2 * HEADS):
                        pool.wait_ge(p_h, n + 1)
                        pool.tensor_tensor(bp_lo[:, :], bs_f[:, :], bp_hi[:, :].bitcast(F32), ALU.subtract).then_inc(p_l, 1)
                        if n + 2 < 2 * HEADS:
                            band_maximum(n + 2)

                    def mix_in(b, t):
                        k = T["o", b, t]
                        pool.wait_ge(free[k % 2], k // 2 + 1)
                        if b == 1:
                            k = T["o", 0, t]
                            pool.wait_ge(free[k % 2], k // 2 + 1)
                        else:
                            pool.wait_ge(mix_add, t + 1)
                        pool.tensor_tensor(mix[:, t, :], mix[:, t, :], gated_at(b, t), ALU.add).then_inc(mix_add, 1)

                    for h in range(HEADS):
                        if h > 1 and h % 2 == 0:
                            mix_in(1, h - 2)
                            mix_in(1, h - 1)
                        pool.wait_ge(z_max, 3 * h + 3)
                        for off in (0, 512, 896, 1024):
                            to = fb[h % 2][:, off:off + P]
                            pool.tensor_tensor(to, to, tri01[:, :], ALU.mult).then_inc(z_mask, 1)
                    mix_in(1, KT - 2)
                    mix_in(1, KT - 1)
                    for t in range(KT):
                        mix_in(2, t)

                    for t in range(KT):
                        pool.wait_ge(scaled_y, t + 1)
                        pool.tensor_tensor(x[:, t, :], x[:, t, :], hf[:, t % 3, :], ALU.add).then_inc(res, 1)
                    for t in range(1, KT, 2):
                        n = KT + t
                        pool.wait_ge(scaled_y, n + 1)
                        pool.tensor_tensor(x[:, t, :], x[:, t, :], hf[:, (n + 1) % 3, :], ALU.add).then_inc(res, 1)

            numbers = [s.num for s in cleared]
            assert numbers == list(range(numbers[0], numbers[0] + len(numbers)))
            nc.all_engine_barrier(sems_to_clear=range(numbers[0], numbers[-1] + 1))

        with nc.Block() as block:

            @block.sync
            def _(sp):
                sp.dma_start(out, x[:, :, :]).then_inc(stored, 16)
                sp.wait_ge(stored, 16)


def constants():
    p, c = np.arange(P)[:, None], np.arange(P)[None, :]
    swap = np.where(p % HEAD < HEAD // 2, p + HEAD // 2, p - HEAD // 2)
    mats = [p == c, swap == c, -(p >= c).astype(np.float32), -np.ones((P, P)), np.ones((P, P)),
            -BIG * (c > p), -BIG * (c >= p), -BIG * (c <= p), p < c]
    const = np.concatenate([np.asarray(m, np.float32) for m in mats], axis=1)

    def inv(d):
        return (1.0 / (np.float32(THETA) ** (np.arange(0, d, 2, dtype=np.float32) / np.float32(d)))).astype(np.float32)

    row = np.arange(P)
    full, part = inv(HEAD)[row % (HEAD // 2)], inv(ROPE_DIM)[row % (ROPE_DIM // 2)]
    sign_full = np.where(row % HEAD < HEAD // 2, -1.0, 1.0)
    sign_part = np.where(row % ROPE_DIM < ROPE_DIM // 2, -1.0, 1.0)
    q, one, zero = 0.25, np.ones(P), np.zeros(P)
    upper = row >= 3 * ROPE_DIM
    trig = [(full, q * one, one), (full, zero, sign_full),
            (part, np.where(upper, 0, q), np.where(upper, sign_part, 1.0)),
            (part, q * one, one), (part, zero, sign_part)]
    cols = [v for f, ph, s in trig for v in (f, ph * 2 * np.pi, zero, s)]
    return const, np.stack(cols, axis=1).astype(np.float32)


def chunk(w, cols):
    w = w[:, cols]
    return w.reshape(-1, P, P).transpose(1, 0, 2).reshape(P, -1)


def weight_stream(w_in, w_uq, w_ukv, w_o, w_out, w_up, w_down):
    r = np.arange
    kr = 384 + r(ROPE_DIM)
    krs = np.roll(kr, ROPE_DIM // 2)
    both = [np.concatenate([64 * t + r(64), 64 * (t + 4) + r(64)]) for t in range(PAIRS)]
    w_o = [w_o[0], w_o[1][np.concatenate(both)], w_o[2]]

    def make(kind, *a):
        if kind == "latent":
            return chunk(w_in, r(P) + P * a[0] if a[0] < 3 else np.concatenate([kr, kr, krs, krs]))
        if kind == "mla":
            h = a[0]
            pe = 96 * h + 64 + r(32)
            q = np.concatenate([96 * h + r(64), pe, np.roll(pe, 16)])
            return np.concatenate([chunk(w_uq, q), chunk(w_ukv, 128 * h + r(128)), np.zeros((P, CH - 3 * P), np.float32)],
                                  axis=1)
        if kind == "swa_k":
            return chunk(w_in, 928 + r(P))
        if kind == "swa_vt":
            return chunk(w_in, 1056 + r(P))
        if kind == "swa_q":
            return chunk(w_in, 416 + both[a[0]])
        if kind in ("stick", "stick_vt"):
            return chunk(w_in, (1184, 1696, 2208)[a[1] if kind == "stick" else 2] + P * a[0] + r(P))
        if kind == "gate":
            return chunk(w_in, 2720 + D * a[0] + P * a[1] + r(P))
        if kind == "o":
            return np.concatenate([chunk(w_o[a[0]], P * t + r(P)) for t in (2 * a[1], 2 * a[1] + 1)], axis=1)
        if kind == "out":
            return chunk(w_out, P * a[0] + r(P))
        if kind == "up":
            return chunk(w_up, D * a[0] + P * a[1] + r(P))
        return chunk(w_down[D * a[0]:D * (a[0] + 1)], P * a[1] + r(P))

    return np.stack([make(*name) for name in C])


def kernel(**inputs):
    import numpy as _np
    import concourse.bacc as _bacc
    from concourse import mybir as _mybir
    from concourse.bass_utils import run_bass_kernel_spmd as _run

    a = {k: _np.asarray(v) for k, v in inputs.items()}
    w = _np.stack([weight_stream(a["w_in"][l], a["w_uq"][l], a["w_ukv"][l],
                                 [a["w_o_mla"][l], a["w_o_swa"][l], a["w_o_sb"][l]],
                                 a["w_out"][l], a["w_up"][l], a["w_down"][l]) for l in range(DEPTH)])
    vecs = []
    for l in range(DEPTH):
        for n in ("g_mix_pre", "b_gate", "g_q_lat", "g_kv_lat", "g_mix_post", "g_mlp_pre", "g_mlp_post"):
            vecs.append(a[n][l].reshape(-1, P).T)
        vecs.append(_np.broadcast_to(a["swa_sinks"][l][None, :], (P, HEADS)))
    const, trig = constants()
    arrays = {
        "x": _np.ascontiguousarray(a["x"][0].T.reshape(KT, P, SEQ).transpose(1, 0, 2)),
        "pos": _np.ascontiguousarray(a["positions"]),
        "w": w, "vec": _np.ascontiguousarray(_np.concatenate(vecs, axis=1)),
        "const": const, "trig": trig,
    }
    nc = _bacc.Bacc("TRN2", target_bir_lowering=False, num_devices=1)
    args = [nc.dram_tensor(f"in_{n}", v.shape, _mybir.dt.from_np(v.dtype), kind="ExternalInput").ap()
            for n, v in arrays.items()]
    out = nc.dram_tensor("out_y", (P, KT, SEQ), F32, kind="ExternalOutput").ap()
    trunk(nc, *args, out)
    r = _run(nc, [{f"in_{n}": v for n, v in arrays.items()}], core_ids=[0])
    got = r.results[0]["out_y"]
    return got.transpose(1, 0, 2).reshape(D, SEQ).T.reshape(1, SEQ, D)
```
